# Optimizing a Trainium2 kernel written in Bass

```python
import math
import jax, jax.numpy as jnp
from jax import lax
import numpy as np

D_MODEL = 1024
BATCH = 1
SEQ = 256
DEPTH = 1

D_MIX = D_MODEL
GLA_HEADS = 4
GLA_DV = (D_MIX // 2) // GLA_HEADS
GLA_DK = GLA_DV // 2
GLA_GATE_RANK = 16
GLA_TAU = 16.0
GLA_CHUNK = 64
MOBA_HEADS = 8
MOBA_HD = (D_MIX - GLA_HEADS * GLA_DV) // MOBA_HEADS
MOBA_BLOCK = 256
MOBA_TOPK = 3
MOBA_QCHUNK = 8
REL_BUCKETS = 32
REL_MAX_DIST = 128
D_FF = 4 * D_MODEL
N_ADA = 6
EPS = 1e-6

GLA_QK_W = GLA_HEADS * GLA_DK
GLA_V_W = GLA_HEADS * GLA_DV
MOBA_W = MOBA_HEADS * MOBA_HD
IN_WIDTHS = (GLA_QK_W, GLA_QK_W, GLA_V_W, GLA_V_W, GLA_GATE_RANK, MOBA_W, MOBA_W, MOBA_W)
D_IN = sum(IN_WIDTHS)
IN_SPLITS = [int(v) for v in np.cumsum(IN_WIDTHS)[:-1]]


def rmsnorm(x, g):
    xf = x.astype(jnp.float32)
    y = xf * lax.rsqrt(jnp.mean(xf * xf, axis=-1, keepdims=True) + EPS)
    return y.astype(x.dtype) * g

def modulate(h, shift, scale):
    return h * (1.0 + scale[:, None, :]) + shift[:, None, :]

def gla_mixer(q, k, v, log_a):
    B, S, H, dk = q.shape
    dv = v.shape[-1]
    C = GLA_CHUNK
    N = S // C
    f32 = jnp.float32

    def chunks(t):
        return t.astype(f32).reshape(B, N, C, H, t.shape[-1]).transpose(0, 3, 1, 2, 4)

    q = chunks(q) * (dk ** -0.5)
    k = chunks(k)
    v = chunks(v)
    g = chunks(log_a)
    b = jnp.cumsum(g, axis=3)
    b_last = b[:, :, :, -1:, :]
    b_ref = b[:, :, :, C // 2 - 1:C // 2, :]
    att = jnp.einsum('bhnid,bhnjd->bhnij', q * jnp.exp(b - b_ref), k * jnp.exp(b_ref - b))
    causal = jnp.tril(jnp.ones((C, C), dtype=bool))
    att = jnp.where(causal, att, 0.0)
    o_intra = jnp.einsum('bhnij,bhnjv->bhniv', att, v)
    kv = jnp.einsum('bhncd,bhncv->bhndv', k * jnp.exp(b_last - b), v)
    decay = jnp.exp(b_last[:, :, :, 0, :])

    def step(s_prev, inp):
        kv_n, dec_n = inp
        return dec_n[..., None] * s_prev + kv_n, s_prev

    s0 = jnp.zeros((B, H, dk, dv), f32)
    _, s_before = lax.scan(step, s0, (kv.transpose(2, 0, 1, 3, 4), decay.transpose(2, 0, 1, 3)))
    s_before = s_before.transpose(1, 2, 0, 3, 4)
    o_inter = jnp.einsum('bhncd,bhndv->bhncv', q * jnp.exp(b), s_before)
    o = o_intra + o_inter
    return o.transpose(0, 2, 3, 1, 4).reshape(B, S, H, dv)

def t5_bucket(rel):
    n = jnp.maximum(rel, 0)
    max_exact = REL_BUCKETS // 2
    ratio = jnp.maximum(n, 1).astype(jnp.float32) / max_exact
    large = max_exact + (jnp.log(ratio) / math.log(REL_MAX_DIST / max_exact)
                         * (REL_BUCKETS - max_exact)).astype(jnp.int32)
    large = jnp.minimum(large, REL_BUCKETS - 1)
    return jnp.where(n < max_exact, n, large)

def moba_mixer(q, k, v, rel_bias):
    B, S, H, hd = q.shape
    BLK = MOBA_BLOCK
    QC = MOBA_QCHUNK
    NB = -(-S // BLK)
    Sp = NB * BLK
    topk = min(MOBA_TOPK, NB)
    f32 = jnp.float32
    qh = q.transpose(0, 2, 1, 3) * (hd ** -0.5)
    pad = ((0, 0), (0, 0), (0, Sp - S), (0, 0))
    kb = jnp.pad(k.transpose(0, 2, 1, 3), pad).reshape(B, H, NB, BLK, hd)
    vb = jnp.pad(v.transpose(0, 2, 1, 3), pad).reshape(B, H, NB, BLK, hd)
    k_mean = jnp.mean(kb.astype(f32), axis=3)
    bias_flat = rel_bias.T.reshape(-1)
    head_off = (jnp.arange(H, dtype=jnp.int32) * REL_BUCKETS)[None, :, None, None]
    blk_pos = jnp.arange(BLK, dtype=jnp.int32)
    blk_ids = jnp.arange(NB, dtype=jnp.int32)
    nq = S // QC
    q_chunks = qh.reshape(B, H, nq, QC, hd).transpose(2, 0, 1, 3, 4)
    gather_blocks = jax.vmap(jax.vmap(lambda kk, ii: kk[ii]))

    def one_chunk(args):
        ci, q_c = args
        t = ci * QC + jnp.arange(QC, dtype=jnp.int32)
        own = (ci * QC) // BLK
        gate = jnp.einsum('bhqd,bhnd->bhqn', q_c.astype(f32), k_mean)
        gate = jnp.where(blk_ids < own, gate, -jnp.inf)
        gval, gidx = lax.top_k(gate, topk)
        valid = jnp.isfinite(gval)
        k_sel = gather_blocks(kb, gidx)
        v_sel = gather_blocks(vb, gidx)
        s_sel = jnp.einsum('bhqd,bhqkld->bhqkl', q_c, k_sel).astype(f32)
        pos_sel = gidx[..., None] * BLK + blk_pos
        rel_sel = t[None, None, :, None, None] - pos_sel
        s_sel = s_sel + bias_flat[head_off[..., None] + t5_bucket(rel_sel)]
        s_sel = jnp.where(valid[..., None], s_sel, -jnp.inf)
        k_own = lax.dynamic_slice_in_dim(kb, own, 1, axis=2)[:, :, 0]
        v_own = lax.dynamic_slice_in_dim(vb, own, 1, axis=2)[:, :, 0]
        s_own = jnp.einsum('bhqd,bhld->bhql', q_c, k_own).astype(f32)
        rel_own = t[:, None] - (own * BLK + blk_pos)[None, :]
        s_own = s_own + bias_flat[head_off + t5_bucket(rel_own)[None, None]]
        s_own = jnp.where(rel_own[None, None] >= 0, s_own, -jnp.inf)
        logits = jnp.concatenate([s_sel.reshape(B, H, QC, topk * BLK), s_own], axis=-1)
        p = jax.nn.softmax(logits, axis=-1)
        p_sel = p[..., :topk * BLK].reshape(B, H, QC, topk, BLK).astype(v.dtype)
        p_own = p[..., topk * BLK:].astype(v.dtype)
        return (jnp.einsum('bhqkl,bhqkld->bhqd', p_sel, v_sel)
                + jnp.einsum('bhql,bhld->bhqd', p_own, v_own))

    out = lax.map(one_chunk, (jnp.arange(nq, dtype=jnp.int32), q_chunks))
    return out.transpose(1, 0, 3, 2, 4).reshape(B, S, H, hd)

def first_inputs(seed: int = 0) -> dict:
    key = jax.random.key(seed)
    ks = jax.random.split(key, 16)
    f32 = jnp.float32
    nrm = lambda k, shape, s: (jax.random.normal(k, shape, f32) * s)
    gain = lambda k, shape: 1.0 + 0.05 * jax.random.normal(k, shape, f32)
    return {
        "x": nrm(ks[0], (BATCH, SEQ, D_MODEL), 1.0),
        "c": nrm(ks[1], (BATCH, D_MODEL), 1.0),
        "w_ada": nrm(ks[2], (DEPTH, D_MODEL, N_ADA * D_MODEL), D_MODEL ** -0.5),
        "b_ada": nrm(ks[3], (DEPTH, N_ADA * D_MODEL), 0.02),
        "g_mix": gain(ks[4], (DEPTH, D_MODEL)),
        "w_in": nrm(ks[5], (DEPTH, D_MODEL, D_IN), D_MODEL ** -0.5),
        "w_gla_gate": nrm(ks[6], (DEPTH, GLA_GATE_RANK, GLA_QK_W), GLA_GATE_RANK ** -0.5),
        "b_gla_gate": nrm(ks[7], (DEPTH, GLA_QK_W), 0.1),
        "g_gla_out": gain(ks[8], (DEPTH, GLA_V_W)),
        "rel_bias": nrm(ks[9], (REL_BUCKETS, MOBA_HEADS), 0.5),
        "w_out": nrm(ks[10], (DEPTH, D_MIX, D_MODEL), D_MIX ** -0.5),
        "g_mlp": gain(ks[11], (DEPTH, D_MODEL)),
        "w_ff1": nrm(ks[12], (DEPTH, D_MODEL, D_FF), D_MODEL ** -0.5),
        "w_ff2": nrm(ks[13], (DEPTH, D_FF, D_MODEL), D_FF ** -0.5),
        "g_final": gain(ks[14], (D_MODEL,)),
    }

def first_block(x, c, w_ada, b_ada, g_mix, w_in, w_gla_gate, b_gla_gate, g_gla_out, rel_bias,
              w_out, g_mlp, w_ff1, w_ff2, g_final):
    B, S, _ = x.shape
    c_act = jax.nn.silu(c)
    for l in range(DEPTH):
        ada = c_act @ w_ada[l] + b_ada[l]
        shift_a, scale_a, gate_a, shift_m, scale_m, gate_m = jnp.split(ada, N_ADA, axis=-1)
        h = modulate(rmsnorm(x, g_mix[l]), shift_a, scale_a)
        proj = h @ w_in[l]
        gq, gk, gv, gr, gg, mq, mk, mv = jnp.split(proj, IN_SPLITS, axis=-1)
        log_a = jax.nn.log_sigmoid((gg @ w_gla_gate[l] + b_gla_gate[l]).astype(jnp.float32)) / GLA_TAU
        o_gla = gla_mixer(gq.reshape(B, S, GLA_HEADS, GLA_DK), gk.reshape(B, S, GLA_HEADS, GLA_DK),
                          gv.reshape(B, S, GLA_HEADS, GLA_DV), log_a.reshape(B, S, GLA_HEADS, GLA_DK))
        o_gla = rmsnorm(o_gla.astype(x.dtype), g_gla_out[l].reshape(GLA_HEADS, GLA_DV))
        o_gla = o_gla.reshape(B, S, GLA_V_W) * jax.nn.silu(gr)
        o_moba = moba_mixer(mq.reshape(B, S, MOBA_HEADS, MOBA_HD), mk.reshape(B, S, MOBA_HEADS, MOBA_HD),
                            mv.reshape(B, S, MOBA_HEADS, MOBA_HD), rel_bias).reshape(B, S, MOBA_W)
        y = jnp.concatenate([o_gla, o_moba], axis=-1) @ w_out[l]
        x = x + gate_a[:, None, :] * y
        h = modulate(rmsnorm(x, g_mlp[l]), shift_m, scale_m)
        x = x + gate_m[:, None, :] * (jnp.square(jax.nn.relu(h @ w_ff1[l])) @ w_ff2[l])
    return rmsnorm(x, g_final)


MIX_WIDTH = D_MODEL
ATTN_WIDTH = MIX_WIDTH // 2
CONV_WIDTH = MIX_WIDTH - ATTN_WIDTH
HEAD_DIM = 64
N_HEADS = ATTN_WIDTH // HEAD_DIM
DILATED_PATTERNS = ((128, 1), (512, 4), (2048, 16))
CONV_KERNEL = 31
N_EXPERTS = 16
CAPACITY_FACTOR = 2
D_FF_EXPERT = 2816
ROPE_THETA = 10000.0
NEG_INF = -1e30
IN_COLS = 3 * ATTN_WIDTH + 2 * CONV_WIDTH


def rms_norm(x, g):
    xf = x.astype(jnp.float32)
    y = xf * lax.rsqrt(jnp.mean(xf * xf, axis=-1, keepdims=True) + EPS)
    return (y * g.astype(jnp.float32)).astype(x.dtype)

def layer_norm(x, g, b):
    xf = x.astype(jnp.float32)
    mu = jnp.mean(xf, axis=-1, keepdims=True)
    xc = xf - mu
    y = xc * lax.rsqrt(jnp.mean(xc * xc, axis=-1, keepdims=True) + EPS)
    return (y * g.astype(jnp.float32) + b.astype(jnp.float32)).astype(x.dtype)

def rope(x, positions):
    half = x.shape[-1] // 2
    inv_freq = ROPE_THETA ** (-jnp.arange(half, dtype=jnp.float32) / half)
    ang = positions.astype(jnp.float32)[:, None] * inv_freq[None, :]
    cos, sin = jnp.cos(ang), jnp.sin(ang)
    xf = x.astype(jnp.float32)
    x1, x2 = xf[..., :half], xf[..., half:]
    out = jnp.concatenate([x1 * cos - x2 * sin, x2 * cos + x1 * sin], axis=-1)
    return out.astype(x.dtype)

def banded_attention(q, k, v, n):
    L, hd = q.shape[-2], q.shape[-1]
    lead = q.shape[:-2]
    nb = -(-L // n)
    Lp = nb * n
    lp = [(0, 0)] * len(lead)
    qb = jnp.pad(q, lp + [(0, Lp - L), (0, 0)]).reshape(*lead, nb, n, hd)

    def windows(t):
        tp = jnp.pad(t, lp + [(n, Lp - L + n), (0, 0)]).reshape(*lead, nb + 2, n, hd)
        return jnp.concatenate([tp[..., 0:nb, :, :], tp[..., 1:nb + 1, :, :],
                                tp[..., 2:nb + 2, :, :]], axis=-2)

    kw, vw = windows(k), windows(v)
    j = jnp.arange(nb)[:, None, None]
    qpos = j * n + jnp.arange(n)[None, :, None]
    kpos = j * n - n + jnp.arange(3 * n)[None, None, :]
    mask = (jnp.abs(qpos - kpos) <= n) & (kpos >= 0) & (kpos < L)
    s = jnp.einsum('...jqd,...jkd->...jqk', qb.astype(jnp.float32),
                   kw.astype(jnp.float32)) * (hd ** -0.5)
    s = jnp.where(mask, s, NEG_INF)
    m = jnp.max(s, axis=-1, keepdims=True)
    p = jnp.exp(s - m)
    l = jnp.sum(p, axis=-1, keepdims=True)
    o = jnp.einsum('...jqk,...jkd->...jqd', p, vw.astype(jnp.float32)) / l
    lse = (m + jnp.log(l))[..., 0]
    o = o.reshape(*lead, Lp, hd)[..., :L, :]
    lse = lse.reshape(*lead, Lp)[..., :L]
    return o, lse

def dilated_attention(q, k, v, window, dilation):
    B, H, S, hd = q.shape
    L = S // dilation

    def split(t):
        return t.reshape(B, H, L, dilation, hd).swapaxes(2, 3)

    o, lse = banded_attention(split(q), split(k), split(v), window // (2 * dilation))
    o = o.swapaxes(2, 3).reshape(B, H, S, hd)
    lse = lse.swapaxes(2, 3).reshape(B, H, S)
    return o, lse

def conformer_conv(a, b, dw_w, dw_b, ln_g, ln_b):
    u = a * jax.nn.sigmoid(b)
    C = u.shape[-1]
    pad = CONV_KERNEL // 2
    u = lax.conv_general_dilated(u, dw_w[:, None, :], window_strides=(1,),
                                 padding=[(pad, pad)],
                                 dimension_numbers=('NWC', 'WIO', 'NWC'),
                                 feature_group_count=C) + dw_b
    u = layer_norm(u, ln_g, ln_b)
    return jax.nn.silu(u)

def expert_choice_moe(h, w_router, w1, w3, w2):
    B, S, D = h.shape
    aff = jax.nn.softmax(jnp.einsum('bsd,de->bse', h, w_router).astype(jnp.float32), axis=-1)
    cap = CAPACITY_FACTOR * S // N_EXPERTS
    gate, idx = lax.top_k(aff.swapaxes(1, 2), cap)
    xe = jax.vmap(lambda hb, ib: hb[ib])(h, idx)

    def expert(args):
        xt, w1e, w3e, w2e = args
        return (jax.nn.silu(xt @ w1e) * (xt @ w3e)) @ w2e

    ye = lax.map(expert, (xe.swapaxes(0, 1), w1, w3, w2))
    ye = ye.swapaxes(0, 1) * gate[..., None].astype(ye.dtype)
    ye = ye.reshape(B, N_EXPERTS * cap, D)
    return jax.vmap(lambda y, i: jnp.zeros((S, D), y.dtype).at[i].add(y))(
        ye, idx.reshape(B, N_EXPERTS * cap))

def second_inputs(seed: int = 0) -> dict:
    key = jax.random.key(seed)
    ks = jax.random.split(key, 16)
    f32 = jnp.float32
    nrm = lambda k, shape, scale: jax.random.normal(k, shape, f32) * scale
    return {
        "x": jax.random.normal(ks[0], (BATCH, SEQ, D_MODEL), f32),
        "norm1_g": 1.0 + nrm(ks[1], (D_MODEL,), 0.02),
        "w_in": nrm(ks[2], (D_MODEL, IN_COLS), D_MODEL ** -0.5),
        "q_norm_g": 1.0 + nrm(ks[3], (HEAD_DIM,), 0.02),
        "k_norm_g": 1.0 + nrm(ks[4], (HEAD_DIM,), 0.02),
        "conv_dw_w": nrm(ks[5], (CONV_KERNEL, CONV_WIDTH), CONV_KERNEL ** -0.5),
        "conv_dw_b": nrm(ks[6], (CONV_WIDTH,), 0.01),
        "conv_ln_g": 1.0 + nrm(ks[7], (CONV_WIDTH,), 0.02),
        "conv_ln_b": nrm(ks[8], (CONV_WIDTH,), 0.01),
        "w_out": nrm(ks[9], (MIX_WIDTH, D_MODEL), MIX_WIDTH ** -0.5),
        "norm2_g": 1.0 + nrm(ks[10], (D_MODEL,), 0.02),
        "w_router": nrm(ks[11], (D_MODEL, N_EXPERTS), D_MODEL ** -0.5),
        "w1": nrm(ks[12], (N_EXPERTS, D_MODEL, D_FF_EXPERT), D_MODEL ** -0.5),
        "w3": nrm(ks[13], (N_EXPERTS, D_MODEL, D_FF_EXPERT), D_MODEL ** -0.5),
        "w2": nrm(ks[14], (N_EXPERTS, D_FF_EXPERT, D_MODEL), D_FF_EXPERT ** -0.5),
    }

def second_block(x, norm1_g, w_in, q_norm_g, k_norm_g, conv_dw_w, conv_dw_b,
              conv_ln_g, conv_ln_b, w_out, norm2_g, w_router, w1, w3, w2):
    B, S, D = x.shape
    positions = jnp.arange(S)
    for _ in range(DEPTH):
        h = rms_norm(x, norm1_g)
        z = jnp.einsum('bsd,dc->bsc', h, w_in)
        A = ATTN_WIDTH

        def heads(t):
            return t.reshape(B, S, N_HEADS, HEAD_DIM).transpose(0, 2, 1, 3)

        q = rope(rms_norm(heads(z[..., 0:A]), q_norm_g), positions)
        k = rope(rms_norm(heads(z[..., A:2 * A]), k_norm_g), positions)
        v = heads(z[..., 2 * A:3 * A])
        outs, lses = [], []
        for window, dilation in DILATED_PATTERNS:
            o_p, lse_p = dilated_attention(q, k, v, window, dilation)
            outs.append(o_p)
            lses.append(lse_p)
        w_mix = jax.nn.softmax(jnp.stack(lses), axis=0)
        attn = jnp.einsum('pbhs,pbhsd->bhsd', w_mix, jnp.stack(outs))
        attn = attn.transpose(0, 2, 1, 3).reshape(B, S, A).astype(x.dtype)

        c0 = 3 * A
        conv = conformer_conv(z[..., c0:c0 + CONV_WIDTH],
                              z[..., c0 + CONV_WIDTH:c0 + 2 * CONV_WIDTH],
                              conv_dw_w, conv_dw_b, conv_ln_g, conv_ln_b)
        mixed = jnp.concatenate([attn, conv.astype(x.dtype)], axis=-1)
        x = x + jnp.einsum('bsc,cd->bsd', mixed, w_out)

        x = x + expert_choice_moe(rms_norm(x, norm2_g), w_router, w1, w3, w2)
    return x


def setup_inputs(seed=0):
    out = dict(first_inputs(seed))
    for name, value in second_inputs(seed + 1).items():
        if name != "x":
            out[name + "_2"] = value
    return out


def reference(
    x, c, w_ada, b_ada, g_mix, w_in, w_gla_gate, b_gla_gate, g_gla_out, rel_bias, w_out, g_mlp,
    w_ff1, w_ff2, g_final, norm1_g_2, w_in_2, q_norm_g_2, k_norm_g_2, conv_dw_w_2, conv_dw_b_2,
    conv_ln_g_2, conv_ln_b_2, w_out_2, norm2_g_2, w_router_2, w1_2, w3_2, w2_2,
):
    x = first_block(
        x, c, w_ada, b_ada, g_mix, w_in, w_gla_gate, b_gla_gate, g_gla_out, rel_bias, w_out,
        g_mlp, w_ff1, w_ff2, g_final,
    )
    return second_block(
        x, norm1_g_2, w_in_2, q_norm_g_2, k_norm_g_2, conv_dw_w_2, conv_dw_b_2, conv_ln_g_2,
        conv_ln_b_2, w_out_2, norm2_g_2, w_router_2, w1_2, w3_2, w2_2,
    )


_drawn_inputs = setup_inputs


def setup_inputs(seed=0):
    import zlib

    import numpy as np

    out = dict(_drawn_inputs(seed))
    spreads = {}
    factors = {'g_gla_out': 2.927,
     'norm1_g_2': 4.692,
     'q_norm_g_2': 8.0,
     'k_norm_g_2': 8.0,
     'conv_dw_b_2': 7.842,
     'conv_ln_g_2': 6.052,
     'conv_ln_b_2': 8.0,
     'norm2_g_2': 4.581}
    for name, (base, spread) in spreads.items():
        noise = np.random.default_rng([zlib.crc32(name.encode()), seed]).standard_normal(out[name].shape)
        drawn = base * np.exp(spread * noise) if base else spread * noise
        out[name] = __import__('jax').numpy.asarray(drawn.astype(out[name].dtype))
    for name, factor in factors.items():
        out[name] = (out[name] * factor).astype(out[name].dtype)
    return out
```

```python
from contextlib import ExitStack

import numpy as np
import concourse.bass as bass
from concourse import mybir

F32 = mybir.dt.float32
ALU = mybir.AluOpType
ACT = mybir.ActivationFunctionType
AX = mybir.AxisListType

P = 128
D = 1024
S = 256
ST = S // P
C = D // P
EPS = 1e-6
NEG = -1e30
GH, GDV, GDK, RANK, CH = 4, 128, 64, 16, 64
NCH = S // CH
QKW, VW = GH * GDK, GH * GDV
MH, HD = 8, 64
MW = MH * HD
FF = 4 * D
BUCKETS = 32
TAPS = 31
PAD = TAPS // 2
CW = 512
CT = CW // P
NE, CAP, FE = 16, 32, 2816
FG = FE // 4
FH = FG // 2
FR = FE // P
DG = D // 4

SLOT = FE
NSLOT = 12
BLOCK = 3 * SLOT
NCHUNK = 24
AR = 14400

UNITS = (["ada0", "ada1", "win_a", "win_b", "win_c", "win_d", "ada2", "ada3", "ada4", "ada5", "wout"]
         + [f"ff1_{u}" for u in range(4)] + [f"ff2_{u}" for u in range(4)]
         + ["conv", "qk", "v", "wo2_0", "wo2_1"])
UNIT = {name: i for i, name in enumerate(UNITS)}
assert (len(UNITS) - 1) % 3 == 2

VEC = {}
for _name, _n in (("b_ada", 48), ("c", 8), ("g_mix", 8), ("g_mlp", 8), ("g_final", 8), ("norm1_g_2", 8),
                  ("norm2_g_2", 8), ("b_gla_gate", 2), ("g_gla_out", 4), ("conv_dw_b_2", 4),
                  ("conv_ln_g_2", 4), ("conv_ln_b_2", 4), ("q_norm_g_2", 1), ("k_norm_g_2", 1)):
    VEC[_name] = (sum(n for _, n in VEC.values()), _n)
NVEC = sum(n for _, n in VEC.values())


def bank_plan():
    order = ["vec", "cw", "rel"] + [f"xr{i}" for i in range(4)] + [f"xn{i}" for i in range(4)]
    order += ["ada0", "ada1", "gg", "gq0", "gq1", "gk0", "gk1", "z"]
    order += [f"wf{i}" for i in range(4)] + ["gv0", "gv1"] + [f"gr{i}" for i in range(4)]
    order += [f"mq{i}" for i in range(4)] + [f"mk{i}" for i in range(4)]
    order += ["klT", "att0", "att1", "kv0", "kv1", "mv0", "mv1", "o0", "o1", "gs0", "gs1"]
    for i in range(MH + 2):
        if i < MH:
            order.append(f"sc{i}")
            if i % 2 == 0:
                order.append(f"ada{2 + i // 2}")
        if 1 <= i <= MH:
            order.append(f"pT{i - 1}")
        if i >= 2 and i % 2 == 0:
            order.append(f"pv{i // 2 - 1}")
    order += ["n_mlp"] + [f"y{m}" for m in range(C)] + [f"f{m}" for m in range(FF // P)]
    held = {"n_mlp": {f"y{m}" for m in range(C)}}
    order += [f"g{m}" for m in range(C)] + ["n_fin", "n_one"]
    for m in range(CT):
        order += [f"cb{m}", f"ca{m}"]
    order += ["qs"] + [f"qk{m}" for m in range(8)] + ["v0", "v1"]
    held["qs"] = {f"qk{m}" for m in range(8)}
    for p in range(4):
        order += [f"bc{p}", f"rt{p}"]
    order += ["cm"]
    for i in range(MH + 2):
        if i < MH:
            order.append(f"tc{i}")
        if 1 <= i <= MH:
            order.append(f"uT{i - 1}")
        if i >= 2 and i % 2 == 0:
            order.append(f"pw{i // 2 - 1}")
    order += ["cv", "n_two"] + [f"z{m}" for m in range(C)]
    held["n_two"] = {f"z{m}" for m in range(C)}
    order += ["lg"] + [f"hn{i}" for i in range(4)] + [f"xf{i}" for i in range(4)] + [f"af{i}" for i in range(8)]
    plan, used, nxt, kept = {}, [0] * 8, 0, {}
    for label in order:
        taken = {b for b, rest in kept.items() if label in rest}
        while nxt % 8 in taken:
            nxt += 1
        if label == "g0":
            nxt = 0
        plan[label] = (nxt % 8, used[nxt % 8])
        used[nxt % 8] += 1
        if label in held:
            kept[nxt % 8] = held[label]
        nxt += 1
    return plan


def build(nc, T, out, rel_dram):
    PLAN = bank_plan()
    with ExitStack() as ctx:
        def sb(name, cols):
            return ctx.enter_context(nc.sbuf_tensor(name, [P, cols], F32))

        def sem(name):
            return ctx.enter_context(nc.semaphore(name))

        ring = sb("ring", NSLOT * SLOT)
        arena = sb("arena", AR)
        xT_ = sb("xT", C * S)
        hT_ = sb("hT", C * S)
        ident = sb("ident", P)
        ones = sb("ones", P)
        cols = sb("cols", NVEC)
        ada = sb("ada", 48)
        cw = sb("cw", CT * TAPS)
        wr = sb("wr", C * NE)
        small = sb("small", 96)
        ps = ctx.enter_context(nc.psum_tensor("ps", [P, 8, 512], F32))

        xT = xT_[:, :].rearrange("p (c s) -> p c s", c=C)
        hT = hT_[:, :].rearrange("p (c s) -> p c s", c=C)
        ext = ring[:, 9 * SLOT:12 * SLOT]

        def ar(off, words, **dims):
            ap = arena[:, off:off + words]
            if dims:
                names = list(dims)
                ap = ap.rearrange(f"p ({' '.join(names)} last) -> p {' '.join(names)} last", **dims)
            return ap

        def ex(off, words, **dims):
            ap = ext[:, off:off + words]
            if dims:
                names = list(dims)
                ap = ap.rearrange(f"p ({' '.join(names)} last) -> p {' '.join(names)} last", **dims)
            return ap

        eps = small[:, 0:1]
        ms = small[:, 1:3]
        rs0 = small[:, 3:5]
        cact = small[:, 8:16]
        amix = small[:, 16:24]
        dec = small[:, 24:32]
        mx = small[:, 32:34]
        mneg = small[:, 34:38]
        rsum = small[:, 38:42]
        rinv = small[:, 42:46]
        amlp = small[:, 48:56]
        sg8 = small[:, 56:64]

        xnat = ar(0, 2048, st=ST)
        xn = ar(2048, 2048, st=ST)
        gv = ar(0, 1024, st=ST)
        gr = ar(1024, 1024, h=GH)
        sgr = ar(2048, 1024, h=GH)
        oT = ar(3072, 1024, h=GH)
        gq, gk, zz, tt, bb, qe, ke, kl, qb = (ar(4096 + 512 * i, 512) for i in range(9))
        klnat = ar(8704, 512)
        att = ar(5120, 1024, h=GH, pair=2)
        qb1 = ar(9216, 512)
        Sst = ar(9728, 768, before=3, pair=2)
        osq = ar(10496, 1024)
        mix = ar(11520, 2048, c=C)
        ggT = arena[0:RANK, 13568:13824]
        wgate = arena[0:RANK, 13824:14080]
        scanm = ar(10496, 512)
        rso = ar(5120, 1024)
        sq1 = ar(8192, 2048, c=C)
        rstd1 = ar(10240, 256)
        h1 = ar(0, 8192, m=FF // P)
        stage = arena[0:NVEC, 4096:4096 + P]
        cwst = arena[0:TAPS, 4224:4224 + CW]
        relst = arena[0:BUCKETS, 4736:4744]
        relW = ex(0, 2048, h=MH)
        relR = ex(2048, 2048, h=MH)
        scb = ex(2048, 768, b=2)
        pTb = ex(2816, 768, b=2)
        mq = ex(3584, 1024, m=4)
        mk = ex(4608, 1024, m=4)
        mv = ex(5632, 1024, st=ST)
        flip = ex(7488, P)
        onehot = ext[0:BUCKETS, 6720:6720 + 384]
        rtb = ext[0:MH, 7104:7104 + 384]

        up = ar(0, 4 * 288, m=CT)
        sgb = ar(1152, 512, b=2)
        qk = ar(1664, 2048, m=8)
        vn = ar(3712, 1024, st=ST)
        mix2 = ar(4736, 2048, c=C)
        C2 = 6784
        cos2, sin2 = ar(C2, 512), ar(C2 + 512, 512)
        cnt2 = ar(C2 + 1024, 512)
        neg2 = ar(9600, 512)
        rot = ar(C2 + 1536, P)
        selh = ar(C2 + 1664, P)
        bsel = arena[0:16, C2 + 1792:C2 + 2816]
        sq2 = ar(10240, 2048, c=C)
        rstd2 = ar(12288, 256)
        tcb = ar(12544, 1024, b=2)
        uTb = ar(10240, 1024, b=2)
        qsq = ar(10240, 512, b=2)
        qt = ar(11264, 1024, b=2)
        rs16 = arena[0:16, 13568:13824]
        lnr = ar(13824, 256)
        csq = ar(0, 1024, m=CT)
        yacc = ar(0, 2048, st=ST)
        hnat = ar(2048, 2048, st=ST)
        junk = ar(4096, 2048)
        C3 = 6784
        lower = ar(C3, 512, st=ST)
        iota = ar(C3 + 512, CAP)
        aff = ar(7400, 32, st=ST)
        rank = ar(7432, 32, st=ST)
        rank2 = ar(7464, 32, st=ST)
        rmx = ar(7496, 2)
        rsm = ar(7498, 2)
        pick = ar(10240, 1024, st=ST)
        xe = ar(12544, 256, c=C)
        sge = ar(4736, 704)
        he = ar(5440, 704)
        hTe = ar(7808, 704, r=FR)
        ye = ar(8512, 256)
        pgs = ar(8768, 256, st=ST)
        pgT = ar(9024, 256)

        filled = [sem(f"bank_filled{b}") for b in range(8)]
        emptied = [sem(f"bank_emptied{b}") for b in range(8)]
        unit_in = [sem(f"unit_in{b}") for b in range(3)]
        unit_in2 = sem("unit_in_gate_columns")
        chunk_in = [sem(f"chunk_in{q}") for q in range(NSLOT)]
        s = {name: sem(name) for name in """
            unit_used x_in vecs_in ident_in ones_set cw_in early_in small_in relW_in eps_set
            act_link dve_link pool_link pe_link cols_set cact_set xn_set amix_set hT_set ggT_set
            gqk_set z_set zl_set b_set e_set gla_set scan_set klnat_set att_set S_set gv_set gr_set
            sgr_set mqk_set mv_set o_set osq_set gla_n mixg_set max_set exp_set p_set pT_set
            mixm_set xmid_set sq1_set n1_set t1_set h_set relu_set x1_set sq2_set n2_set xf_set
            sqf_set n3_set h2_set consts2_in neg_set sgb_set up_set conv_set qk_set qsq_set rs16_set
            qn_set rt_set qf_set v_set cmean_set csq_set cvar_set cln_set csg_set mixc_set tmax_set
            texp_set tp_set uT_set mixa_set x2_set sq3_set n4_set h3_set hnat_set yinit_set
            consts3_in lg_set lge_set aff_set rank_set pick_set w_used xe_full xe_set h1_full
            h3_full sg_set he_set hTe_set ye_full ye_set pgs_set pgT_full pgT_set sc_full sc_used
            y_done out_done rtbneg_set rs16i_set qb1z_set attz_set attd_set upz_set xr_set
            rel_dram_in adacol_set hid_used""".split()}

        def bk(label):
            return ps[:, PLAN[label][0], :]

        def wait_filled(eng, label):
            b, n = PLAN[label]
            eng.wait_ge(filled[b], n + 1)

        def wait_emptied(eng, label):
            b, n = PLAN[label]
            if n:
                eng.wait_ge(emptied[b], n)

        def inc_filled(ins, label):
            ins.then_inc(filled[PLAN[label][0]], 1)

        def inc_emptied(ins, label):
            ins.then_inc(emptied[PLAN[label][0]], 1)

        def empty(eng, label):
            eng.sem_inc(emptied[PLAN[label][0]], 1)

        def wait_unit(eng, name):
            i = UNIT[name]
            eng.wait_ge(unit_in[i % 3], 16 * (i // 3 + 1))

        def unit_ap(name, k, n):
            o = (UNIT[name] % 3) * BLOCK
            return ring[:, o:o + k * n].rearrange("p (k n) -> p k n", k=k)

        def vcol(name, i):
            return cols[:, VEC[name][0] + i:VEC[name][0] + i + 1]

        def flat(ap):
            return ap.rearrange("p a b -> p (a b)")

        block = ctx.enter_context(nc.Block())

        @block.sync
        def _(sp):
            def rows(ap, c0, n):
                return ap[:, c0:c0 + n].rearrange("(c p) n -> p c n", p=P)

            def unit_source(name):
                if name.startswith("ada"):
                    return rows(T["w_ada"], D * int(name[3]), D)
                if name.startswith("win_"):
                    c0, n = {"a": (0, 2 * QKW), "b": (512, 1024), "c": (1552, 1024), "d": (2576, 512)}[name[4]]
                    return rows(T["w_in"], c0, n)
                if name == "wout":
                    return rows(T["w_out"], 0, D)
                if name.startswith("ff1"):
                    return rows(T["w_ff1"], D * int(name[4]), D)
                if name.startswith("ff2"):
                    u = int(name[4])
                    return rows(T["w_ff2"][u * D:(u + 1) * D, :], 0, D)
                if name in ("conv", "qk", "v"):
                    c0, n = {"conv": (3 * MW, 2 * CW), "qk": (0, 2 * MW), "v": (2 * MW, MW)}[name]
                    return rows(T["w_in_2"], c0, n)
                return rows(T["w_out_2"], 512 * int(name[4]), 512)

            for i, name in enumerate(UNITS):
                if i >= 3:
                    sp.wait_ge(s["unit_used"], i - 2)
                src = unit_source(name)
                sp.dma_start(unit_ap(name, C, src.shape[2]), src).then_inc(unit_in[i % 3], 16)
                if name == "win_a":
                    o = (i % 3) * BLOCK + C * 512
                    sp.dma_start(ring[:, o:o + C * RANK].rearrange("p (c n) -> p c n", c=C),
                                 rows(T["w_in"], 1536, RANK)).then_inc(unit_in2, 16)

            w1 = T["w1_2"].rearrange("e (c p) f -> p e c f", p=P)
            w3 = T["w3_2"].rearrange("e (c p) f -> p e c f", p=P)
            w2 = T["w2_2"].rearrange("e (p r) n -> p e (r n)", r=FR)

            def chunk(e, q):
                slot = (9 + q) % NSLOT
                if q < C:
                    src = w1[:, e, q, :]
                elif q < 2 * C:
                    src = w3[:, e, q - C, :]
                else:
                    src = w2[:, e, (q - 2 * C) * SLOT:(q - 2 * C + 1) * SLOT]
                sp.dma_start(ring[:, slot * SLOT:(slot + 1) * SLOT], src).then_inc(chunk_in[slot], 16)

            for q in range(NSLOT):
                if q == 0:
                    sp.wait_ge(s["unit_used"], UNIT["wout"] + 1)
                elif q % 3 == 0:
                    sp.wait_ge(s["unit_used"], len(UNITS) - 3 + q // 3)
                chunk(0, q)
            with sp.Fori(0, NE - 1) as e:
                for q in range(NCHUNK):
                    if q != 4:
                        sp.wait_ge(s["w_used"], NCHUNK * e + q + 1 + (q == 3))
                    if q < NSLOT:
                        chunk(e, q + NSLOT)
                    else:
                        chunk(e + 1, q - NSLOT)
            for q in range(NSLOT):
                sp.wait_ge(s["w_used"], NCHUNK * (NE - 1) + q + 1)
                chunk(NE - 1, q + NSLOT)

        @block.gpsimd
        def _(pool):
            nc.gpsimd.memset(ones[:, :], 1.0).then_inc(s["ones_set"], 1)
            nc.gpsimd.memset(eps, EPS).then_inc(s["eps_set"], 1)
            nc.gpsimd.memset(scanm, 1.0).then_inc(s["pool_link"], 1)
            pool.wait_ge(s["pool_link"], 1)
            nc.gpsimd.memset(scanm.rearrange("p (n t) -> p n t", t=CH)[:, :, 0:1], 0.0).then_inc(s["scan_set"], 1)
            nc.gpsimd.memset(qb1, 0.0).then_inc(s["qb1z_set"], 1)
            pool.wait_ge(s["e_set"], 4)
            nc.gpsimd.memset(ar(5120, 1024), 0.0).then_inc(s["attz_set"], 1)
            pool.wait_ge(s["attd_set"], 4)
            for h in range(GH):
                nc.gpsimd.affine_select(out=att[:, h, :, :], in_=att[:, h, :, :], compare_op=ALU.is_ge, fill=0.0,
                                        base=0, pattern=[[0, 2], [1, P]], channel_multiplier=-1).then_inc(s["att_set"], 1)
            pool.wait_ge(s["hid_used"], 1)
            pool.dma_start(ar(C2, 1792), T["table2"][:, 0:1792]).then_inc(s["consts2_in"], 16)
            pool.dma_start(bsel, T["table2"][0:16, 1792:2816]).then_inc(s["consts2_in"], 16)
            nc.gpsimd.memset(ar(0, 4 * 288), 0.0).then_inc(s["upz_set"], 1)
            pool.wait_ge(s["consts2_in"], 32)
            nc.gpsimd.tensor_scalar(neg2, cnt2, 0.0, NEG, ALU.is_equal, ALU.mult).then_inc(s["neg_set"], 1)
            pool.wait_ge(s["tp_set"], MH)
            pool.dma_start(ar(C3, 512 + CAP), T["table3"]).then_inc(s["consts3_in"], 16)

            pool.wait_ge(s["pick_set"], 1)
            with pool.Fori(0, NE) as e:
                pool.wait_ge(s["pgT_full"], 1 + e)
                for st in range(ST):
                    ins = nc.gpsimd.tensor_tensor(
                        pgs[:, st, :].rearrange("p (j t) -> p j t", j=4),
                        pick[:, st, bass.ds(e * CAP, CAP)].unsqueeze(1).broadcast_to([P, 4, CAP]),
                        aff[:, st, bass.ds(e, 1)].unsqueeze(1).broadcast_to([P, 4, CAP]), ALU.mult)
                ins.then_inc(s["pgs_set"], 1)

        @block.scalar
        def _(act):
            n_link = [0]

            def link(ins):
                n_link[0] += 1
                ins.then_inc(s["act_link"], 1)
                act.wait_ge(s["act_link"], n_link[0])

            A = nc.scalar.activation
            x_rows = T["x"].rearrange("b (st p) d -> p (b st) d", p=P)
            act.dma_start(xnat, x_rows).then_inc(s["x_in"], 16)
            act.dma_start(ident[:, :], T["table1"][:, 0:P]).then_inc(s["ident_in"], 16)
            for name, (r0, n) in VEC.items():
                v = T[name]
                if name in ("q_norm_g_2", "k_norm_g_2"):
                    for half in range(2):
                        act.dma_start(stage[r0:r0 + 1, HD * half:HD * half + HD],
                                      v.rearrange("(a n) -> a n", a=1)).then_inc(s["vecs_in"], 16)
                    continue
                v = v.rearrange("a n -> (a n)") if len(v.shape) == 2 else v
                act.dma_start(stage[r0:r0 + n, :], v.rearrange("(r n) -> r n", n=P)).then_inc(s["vecs_in"], 16)
            act.dma_start(cwst, T["conv_dw_w_2"]).then_inc(s["cw_in"], 16)
            act.dma_start(relst, T["rel_bias"]).then_inc(s["early_in"], 16)
            act.dma_start(onehot, T["table1"][0:BUCKETS, P:P + 384]).then_inc(s["early_in"], 16)
            act.dma_start(flip, T["table1"][:, P + 384:]).then_inc(s["early_in"], 16)
            act.dma_start(wgate, T["w_gla_gate"]).then_inc(s["small_in"], 16)
            act.dma_start(wr[:, :].rearrange("p (c e) -> p c e", c=C),
                          T["w_router_2"].rearrange("(c p) e -> p c e", p=P)).then_inc(s["small_in"], 16)

            act.wait_ge(s["x_in"], 16)
            act.wait_ge(s["eps_set"], 1)
            for st in range(ST):
                last = A(xn[:, st, :], xnat[:, st, :], ACT.Square, accum_out=ms[:, st:st + 1])
            link(last)
            A(ms, ms, ACT.Sqrt, bias=eps, scale=1.0 / D).then_inc(s["xn_set"], 1)
            act.wait_ge(s["cols_set"], 1)
            A(sg8, cols[:, VEC["c"][0]:VEC["c"][0] + C], ACT.Sigmoid).then_inc(s["cact_set"], 1)
            wait_filled(act, "rel")
            inc_emptied(A(rtb[:, 0:S], bk("rel")[0:MH, 0:S], ACT.Copy), "rel")
            act.wait_ge(emptied[PLAN["rel"][0]], PLAN["rel"][1] + 1)
            act.wait_ge(s["rtbneg_set"], 1)
            act.dma_start(rel_dram, rtb).then_inc(s["rel_dram_in"], 16)
            act.wait_ge(s["rel_dram_in"], 16)
            act.dma_start(relR, bass.AP(rel_dram.tensor, 0, [[1, P], [384, MH], [1, S]])).then_inc(s["relW_in"], 16)

            act.wait_ge(s["amix_set"], 1)
            for c in range(C):
                if c % 2 == 0:
                    wait_filled(act, f"xn{c // 2}")
                ins = A(hT[:, c, :], bk(f"xn{c // 2}")[:, (c % 2) * S:(c % 2) * S + S], ACT.Identity,
                        scale=amix[:, c:c + 1], bias=ada[:, c:c + 1])
                ins.then_inc(s["hT_set"], 1)
                if c % 2:
                    act.wait_ge(s["hT_set"], c + 1)
                    empty(act, f"xn{c // 2}")

            def evac(label, dst, src, done, func=ACT.Copy, **kw):
                wait_filled(act, label)
                A(dst, src, func, **kw).then_inc(done, 1)

            free_n = [0]

            def take(label, dst, src, done, n, func=ACT.Copy, **kw):
                evac(label, dst, src, done, func, **kw)
                act.wait_ge(done, n)
                empty(act, label)

            take("gg", ggT, bk("gg")[0:RANK, 0:S], s["ggT_set"], 1)
            take("gq0", gq[:, 0:S], bk("gq0")[:, 0:S], s["gqk_set"], 1)
            take("gq1", gq[:, S:2 * S], bk("gq1")[:, 0:S], s["gqk_set"], 2)
            take("gk0", gk[:, 0:S], bk("gk0")[:, 0:S], s["gqk_set"], 3)
            take("gk1", gk[:, S:2 * S], bk("gk1")[:, 0:S], s["gqk_set"], 4)
            wait_filled(act, "z")
            for mt in range(2):
                last = A(zz[:, mt * S:(mt + 1) * S], bk("z")[:, mt * S:(mt + 1) * S], ACT.Identity,
                         bias=vcol("b_gla_gate", mt))
                last.then_inc(s["z_set"], 1)
            act.wait_ge(s["z_set"], 2)
            empty(act, "z")
            link(A(tt, zz, ACT.Abs))
            link(A(tt, tt, ACT.Exp, scale=-1.0))
            A(tt, tt, ACT.Ln, bias=1.0).then_inc(s["zl_set"], 1)
            take("gv0", gv[:, 0, :], bk("gv0"), s["gv_set"], 1)
            take("gv1", gv[:, 1, :], bk("gv1"), s["gv_set"], 2)
            for h in range(GH):
                wait_filled(act, f"gr{h}")
                A(gr[:, h, :], bk(f"gr{h}")[:, 0:S], ACT.Copy).then_inc(s["gr_set"], 1)
                act.wait_ge(s["gr_set"], h + 1)
                empty(act, f"gr{h}")
            A(flat(sgr), flat(gr), ACT.Sigmoid).then_inc(s["sgr_set"], 1)
            act.wait_ge(s["b_set"], 3)
            T16 = 1.0 / 16
            A(qe, zz, ACT.Exp, scale=T16).then_inc(s["e_set"], 1)
            A(ke, zz, ACT.Exp, scale=-T16).then_inc(s["e_set"], 1)
            A(kl, tt, ACT.Exp, scale=T16).then_inc(s["e_set"], 1)
            A(qb, bb, ACT.Exp, scale=T16).then_inc(s["e_set"], 1)
            A(dec, bb.rearrange("p (n t) -> p n t", t=CH)[:, :, CH - 1], ACT.Exp, scale=T16).then_inc(s["e_set"], 1)
            for m in range(4):
                take(f"mq{m}", mq[:, m, :], bk(f"mq{m}")[:, 0:S], s["mqk_set"], m + 1)
            for m in range(4):
                take(f"mk{m}", mk[:, m, :], bk(f"mk{m}")[:, 0:S], s["mqk_set"], 5 + m)
            take("klT", klnat, bk("klT"), s["klnat_set"], 1)
            act.wait_ge(s["attz_set"], 1)
            for par in range(2):
                wait_filled(act, f"att{par}")
                for np_ in (0, CH):
                    A(att[np_:np_ + CH, par::2, :, np_:np_ + CH],
                      bk(f"att{par}")[np_:np_ + CH, 0:2 * 2 * CH].rearrange("p (h pair q) -> p h pair q", h=2, pair=2),
                      ACT.Copy).then_inc(s["attd_set"], 1)
                act.wait_ge(s["attd_set"], 2 * par + 2)
                empty(act, f"att{par}")
            take("mv0", mv[:, 0, :], bk("mv0"), s["mv_set"], 1)
            take("mv1", mv[:, 1, :], bk("mv1"), s["mv_set"], 2)
            for i in range(2):
                wait_filled(act, f"o{i}")
                A(flat(oT[:, 2 * i:2 * i + 2, :]), bk(f"o{i}"), ACT.Copy).then_inc(s["o_set"], 1)
                A(osq[:, i * 512:(i + 1) * 512], bk(f"o{i}"), ACT.Square).then_inc(s["osq_set"], 1)
                act.wait_ge(s["o_set"], i + 1)
                act.wait_ge(s["osq_set"], i + 1)
                empty(act, f"o{i}")
            for i in range(2):
                take(f"gs{i}", rso[:, i * 512:(i + 1) * 512], bk(f"gs{i}"), s["gla_n"], i + 1, ACT.Sqrt,
                     bias=eps, scale=1.0 / GDV)
            for i in range(MH + 1):
                if i < MH:
                    act.wait_ge(s["max_set"], i + 1)
                    b = i % 2
                    for st in range(ST):
                        sl = scb[:, b, 0:P] if st == 0 else scb[:, b, P:P + S]
                        A(sl, sl, ACT.Exp, bias=mneg[:, 2 * b + st:2 * b + st + 1],
                          accum_out=rsum[:, 2 * b + st:2 * b + st + 1]).then_inc(s["exp_set"], 1)
                if i >= 1:
                    j = i - 1
                    if j >= 2:
                        act.wait_ge(filled[PLAN[f"pv{(j - 2) // 2}"][0]], PLAN[f"pv{(j - 2) // 2}"][1] + 1)
                    take(f"pT{j}", pTb[:, j % 2, :], bk(f"pT{j}")[:, 0:384], s["pT_set"], j + 1)

            def squares(ready, dst, n0, done):
                for c in range(C):
                    act.wait_ge(ready, n0 + c + 1)
                    A(dst[:, c, :], xT[:, c, :], ACT.Square).then_inc(done, 1)

            def root(label, dst, done):
                wait_filled(act, label)
                A(dst, bk(label)[:, 0:S], ACT.Sqrt, bias=eps, scale=1.0 / D).then_inc(done, 1)
                act.wait_ge(done, 1)
                empty(act, label)

            squares(s["xmid_set"], sq1, 0, s["sq1_set"])
            root("n_mlp", rstd1, s["n1_set"])
            for c in range(C):
                act.wait_ge(s["t1_set"], c + 1)
                A(hT[:, c, :], hT[:, c, :], ACT.Identity, bias=ada[:, 24 + c:25 + c]).then_inc(s["h_set"], 1)
            for m in range(FF // P):
                wait_filled(act, f"f{m}")
                A(h1[:, m, :], bk(f"f{m}")[:, 0:S], ACT.Relu).then_inc(s["relu_set"], 1)
                act.wait_ge(s["relu_set"], m + 1)
                inc_emptied(A(h1[:, m, :], h1[:, m, :], ACT.Square), f"f{m}")
            squares(s["x1_set"], sq2, 0, s["sq2_set"])
            root("n_fin", rstd2, s["n2_set"])
            act.wait_ge(s["xf_set"], C)
            squares(s["xf_set"], sq2, 0, s["sqf_set"])
            root("n_one", rstd2, s["n3_set"])
            for m in range(CT):
                wait_filled(act, f"cb{m}")
                if m >= 2:
                    act.wait_ge(s["up_set"], m - 1)
                take(f"cb{m}", sgb[:, m % 2, :], bk(f"cb{m}")[:, 0:S], s["sgb_set"], m + 1, ACT.Sigmoid)
            for m in range(8):
                if m >= 2:
                    act.wait_ge(s["pe_link"], m - 1)
                wait_filled(act, f"qk{m}")
                A(qsq[:, m % 2, :], bk(f"qk{m}")[:, 0:S], ACT.Square).then_inc(s["qsq_set"], 1)
                A(qk[:, m, :], bk(f"qk{m}")[:, 0:S], ACT.Copy).then_inc(s["qk_set"], 1)
                act.wait_ge(s["qk_set"], m + 1)
                act.wait_ge(s["qsq_set"], m + 1)
                empty(act, f"qk{m}")
            wait_filled(act, "qs")
            A(rs16, bk("qs")[0:16, 0:S], ACT.Sqrt, bias=eps[0:16, :], scale=1.0 / HD).then_inc(s["rs16_set"], 1)
            act.wait_ge(s["rs16_set"], 1)
            empty(act, "qs")
            take("v0", vn[:, 0, :], bk("v0"), s["v_set"], 1)
            take("v1", vn[:, 1, :], bk("v1"), s["v_set"], 2)
            for i in range(MH + 1):
                if i < MH:
                    act.wait_ge(s["tmax_set"], i + 1)
                    b = i % 2
                    for st in range(ST):
                        sl = tcb[:, b, st * S:(st + 1) * S]
                        A(sl, sl, ACT.Exp, bias=mneg[:, 2 * b + st:2 * b + st + 1]).then_inc(s["texp_set"], 1)
                if i >= 1:
                    j = i - 1
                    if j >= 2:
                        act.wait_ge(filled[PLAN[f"pw{(j - 2) // 2}"][0]], PLAN[f"pw{(j - 2) // 2}"][1] + 1)
                    take(f"uT{j}", uTb[:, j % 2, :], bk(f"uT{j}"), s["uT_set"], j + 1)
            act.wait_ge(s["cmean_set"], CT)
            A(flat(csq), flat(mix2[:, 4:8, :]), ACT.Square).then_inc(s["csq_set"], 1)
            wait_filled(act, "cv")
            A(lnr, bk("cv")[:, 0:S], ACT.Sqrt, bias=eps, scale=1.0 / CW).then_inc(s["cvar_set"], 1)
            act.wait_ge(s["cvar_set"], 1)
            empty(act, "cv")
            act.wait_ge(s["cln_set"], CT)
            A(flat(csq), flat(mix2[:, 4:8, :]), ACT.Sigmoid).then_inc(s["csg_set"], 1)
            squares(s["x2_set"], sq2, 0, s["sq3_set"])
            root("n_two", rstd2, s["n4_set"])
            for i in range(4):
                wait_filled(act, f"hn{i}")
                for st in range(ST):
                    src = bk(f"hn{i}").rearrange("p (c st d) -> p c st d", c=2, st=ST)[:, :, st, :]
                    A(hnat[:, st, 2 * i * P:(2 * i + 2) * P].rearrange("p (c d) -> p c d", c=2), src,
                      ACT.Copy).then_inc(s["hnat_set"], 1)
                act.wait_ge(s["hnat_set"], 2 * i + 2)
                empty(act, f"hn{i}")
            for i in range(4):
                wait_filled(act, f"xf{i}")
                for st in range(ST):
                    src = bk(f"xf{i}").rearrange("p (c st d) -> p c st d", c=2, st=ST)[:, :, st, :]
                    A(yacc[:, st, 2 * i * P:(2 * i + 2) * P].rearrange("p (c d) -> p c d", c=2), src,
                      ACT.Copy).then_inc(s["yinit_set"], 1)
                act.wait_ge(s["yinit_set"], 2 * i + 2)
                empty(act, f"xf{i}")
            act.wait_ge(s["lg_set"], 1)
            A(flat(aff), flat(aff), ACT.Exp).then_inc(s["lge_set"], 1)

            act.sem_inc(s["xe_set"], 1)
            act.sem_inc(s["ye_set"], 1)
            with act.Fori(0, NE) as e:
                act.wait_ge(s["xe_full"], e + 1)
                A(flat(xe), ps[:, 7, 0:S], ACT.Copy).then_inc(s["xe_set"], 1)
                act.wait_ge(s["pgT_full"], e + 2)
                act.wait_ge(s["sc_full"], 1 + 4 * e)
                A(pgT, ps[:, 4, 0:S], ACT.Copy).then_inc(s["pgT_set"], 1)
                act.wait_ge(s["h1_full"], e + 1)
                act.wait_ge(s["he_set"], 1 + 2 * e)
                A(sge.rearrange("p (a b) -> p a b", a=2), ps[:, 0:2, 0:FH], ACT.Sigmoid).then_inc(s["sg_set"], 1)
                act.wait_ge(s["ye_full"], e + 1)
                A(ye, ps[:, 4, 0:DG], ACT.Copy).then_inc(s["ye_set"], 1)
            act.wait_ge(s["y_done"], 4)
            o_rows = out.rearrange("b (st p) d -> p (b st) d", p=P)
            act.dma_start(o_rows, yacc).then_inc(s["out_done"], 16)
            act.wait_ge(s["out_done"], 16)

        @block.vector
        def _(dve):
            V = nc.vector
            n_link = [0]

            def link(ins):
                n_link[0] += 1
                ins.then_inc(s["dve_link"], 1)
                dve.wait_ge(s["dve_link"], n_link[0])

            wait_filled(dve, "vec")
            inc_emptied(V.tensor_copy(cols[:, :], bk("vec")[:, 0:NVEC]), "vec")
            dve.wait_ge(emptied[PLAN["vec"][0]], PLAN["vec"][1] + 1)
            dve.sem_inc(s["cols_set"], 1)
            wait_filled(dve, "cw")
            inc_emptied(V.tensor_copy(cw[:, :].rearrange("p (m k) -> p m k", m=CT),
                                      bk("cw").rearrange("p (m k) -> p m k", m=CT)[:, :, 0:TAPS]), "cw")
            dve.wait_ge(s["xn_set"], 1)
            link(V.reciprocal(rs0, ms))
            for st in range(ST):
                V.tensor_scalar(xn[:, st, :], xnat[:, st, :], rs0[:, st:st + 1], None, ALU.mult).then_inc(s["xr_set"], 1)
            dve.wait_ge(s["cact_set"], 1)
            V.tensor_tensor(cact, sg8, cols[:, VEC["c"][0]:VEC["c"][0] + C], ALU.mult).then_inc(s["adacol_set"], 1)
            V.memset(rtb[:, S:384], NEG).then_inc(s["rtbneg_set"], 1)
            for i in range(4):
                wait_filled(dve, f"xr{i}")
                inc_emptied(V.tensor_copy(flat(xT[:, 2 * i:2 * i + 2, :]), bk(f"xr{i}")), f"xr{i}")

            def take_ada(k):
                wait_filled(dve, f"ada{k}")
                b0 = VEC["b_ada"][0] + C * k
                inc_emptied(V.tensor_tensor(ada[:, C * k:C * k + C], bk(f"ada{k}")[:, 0:C], cols[:, b0:b0 + C],
                                            ALU.add), f"ada{k}")
                dve.wait_ge(emptied[PLAN[f"ada{k}"][0]], PLAN[f"ada{k}"][1] + 1)

            take_ada(0)
            take_ada(1)
            g0 = VEC["g_mix"][0]
            V.scalar_tensor_tensor(amix, ada[:, C:2 * C], 1.0, cols[:, g0:g0 + C], ALU.add, ALU.mult)\
                .then_inc(s["amix_set"], 1)

            for i in range(4):
                wait_filled(dve, f"wf{i}")
                inc_emptied(V.tensor_copy(flat(relW[:, 2 * i:2 * i + 2, :]), bk(f"wf{i}")), f"wf{i}")
            dve.wait_ge(s["zl_set"], 1)
            link(V.scalar_tensor_tensor(zz, zz, 0.0, tt, ALU.min, ALU.subtract))
            dve.wait_ge(s["scan_set"], 1)
            link(V.tensor_tensor_scan(bb, scanm, zz, 0.0, ALU.mult, ALU.add))
            b3, z3, t3 = (a.rearrange("p (n t) -> p n t", t=CH) for a in (bb, zz, tt))
            V.tensor_tensor(z3, b3, b3[:, :, CH // 2 - 1:CH // 2].broadcast_to([P, 2 * NCH, CH]), ALU.subtract)\
                .then_inc(s["b_set"], 1)
            V.tensor_tensor(t3, b3[:, :, CH - 1:CH].broadcast_to([P, 2 * NCH, CH]), b3, ALU.subtract)\
                .then_inc(s["b_set"], 1)
            dve.wait_ge(s["b_set"], 2)
            dve.sem_inc(s["b_set"], 1)
            dve.wait_ge(s["e_set"], 4)
            dve.wait_ge(s["gqk_set"], 4)
            V.scalar_tensor_tensor(qe, qe, GDK ** -0.5, gq, ALU.mult, ALU.mult).then_inc(s["gla_set"], 1)
            V.tensor_tensor(ke, ke, gk, ALU.mult).then_inc(s["gla_set"], 1)
            V.tensor_tensor(kl, kl, gk, ALU.mult).then_inc(s["gla_set"], 1)
            dve.wait_ge(s["qb1z_set"], 1)
            V.scalar_tensor_tensor(qb1[CH:P, :], qb[CH:P, :], GDK ** -0.5, gq[CH:P, :], ALU.mult, ALU.mult)\
                .then_inc(s["gla_set"], 1)
            V.scalar_tensor_tensor(qb[0:CH, :], qb[0:CH, :], GDK ** -0.5, gq[0:CH, :], ALU.mult, ALU.mult)\
                .then_inc(s["gla_set"], 1)
            dve.wait_ge(s["gla_set"], 5)
            V.memset(qb[CH:P, :], 0.0).then_inc(s["gla_set"], 1)
            dve.wait_ge(s["sgr_set"], 1)
            link(V.tensor_tensor(flat(gr), flat(gr), flat(sgr), ALU.mult))
            wait_filled(dve, "kv0")
            kv0 = bk("kv0").rearrange("p (n m v) -> p n m v", n=2, m=2)
            kv1 = bk("kv1")[:, 0:S].rearrange("p (m v) -> p m v", m=2)
            link(V.tensor_copy(Sst[:, 0, :, :], kv0[:, 0, :, :]))
            dve.wait_ge(s["e_set"], 5)
            wait_filled(dve, "kv1")
            for mt in range(2):
                link(V.scalar_tensor_tensor(S_at(Sst, 1, mt), S_at(Sst, 0, mt), dec[:, NCH * mt + 1:NCH * mt + 2],
                                            kv1[:, mt, :], ALU.mult, ALU.add))
            empty(dve, "kv1")
            for mt in range(2):
                link(V.scalar_tensor_tensor(S_at(Sst, 2, mt), S_at(Sst, 1, mt), dec[:, NCH * mt + 2:NCH * mt + 3],
                                            kv0[:, 1, mt, :], ALU.mult, ALU.add))
            empty(dve, "kv0")
            dve.sem_inc(s["S_set"], 1)
            def gla_finish():
                for i in range(2):
                    dve.wait_ge(s["gla_n"], i + 1)
                    link(V.reciprocal(rso[:, i * 512:(i + 1) * 512], rso[:, i * 512:(i + 1) * 512]))
                    for h in (2 * i, 2 * i + 1):
                        link(V.scalar_tensor_tensor(oT[:, h, :], oT[:, h, :], vcol("g_gla_out", h),
                                                    rso[:, h * S:(h + 1) * S], ALU.mult, ALU.mult))
                        V.tensor_tensor(mix[:, h, :], oT[:, h, :], gr[:, h, :], ALU.mult).then_inc(s["mixg_set"], 1)

            dve.wait_ge(emptied[PLAN["wf3"][0]], PLAN["wf3"][1] + 1)
            for i in range(MH + 2):
                if i < MH:
                    b = i % 2
                    wait_filled(dve, f"sc{i}")
                    if i >= 2:
                        wait_filled(dve, f"pT{i - 2}")
                    V.scalar_tensor_tensor(scb[:, b, 0:P], bk(f"sc{i}")[:, 0:P], HD ** -0.5, relW[:, i, P:2 * P],
                                           ALU.mult, ALU.add)
                    link(V.scalar_tensor_tensor(scb[:, b, P:P + S], bk(f"sc{i}")[:, P:P + S], HD ** -0.5,
                                                relW[:, i, :], ALU.mult, ALU.add))
                    V.reduce_max(mx[:, 0:1], scb[:, b, 0:P], AX.X)
                    link(V.reduce_max(mx[:, 1:2], scb[:, b, P:P + S], AX.X))
                    empty(dve, f"sc{i}")
                    V.tensor_scalar(mneg[:, 2 * b:2 * b + 2], mx, -1.0, None, ALU.mult).then_inc(s["max_set"], 1)
                    if i % 2 == 0:
                        take_ada(2 + i // 2)
                if 1 <= i <= MH:
                    b = (i - 1) % 2
                    dve.wait_ge(s["exp_set"], 2 * i)
                    link(V.reciprocal(rinv[:, 2 * b:2 * b + 2], rsum[:, 2 * b:2 * b + 2]))
                    V.tensor_scalar(scb[:, b, 0:P], scb[:, b, 0:P], rinv[:, 2 * b:2 * b + 1], None, ALU.mult)
                    V.tensor_scalar(scb[:, b, P:P + S], scb[:, b, P:P + S], rinv[:, 2 * b + 1:2 * b + 2], None,
                                    ALU.mult).then_inc(s["p_set"], 1)
                if i == 1:
                    gla_finish()
                if i >= 2 and i % 2 == 0:
                    p = i // 2 - 1
                    pass
                if i >= 3 and i % 2 == 1:
                    p = (i - 3) // 2
                    wait_filled(dve, f"pv{p}")
                    inc_emptied(V.tensor_copy(mix[:, 4 + p, :], bk(f"pv{p}")[:, 0:S]), f"pv{p}")
                    dve.wait_ge(emptied[PLAN[f"pv{p}"][0]], PLAN[f"pv{p}"][1] + 1)
                    dve.sem_inc(s["mixm_set"], 1)
            g1 = VEC["g_mlp"][0]
            link(V.scalar_tensor_tensor(amlp, ada[:, 4 * C:5 * C], 1.0, cols[:, g1:g1 + C], ALU.add, ALU.mult))

            def add_gated(label, gate, done):
                for m in range(C):
                    wait_filled(dve, f"{label}{m}")
                    V.scalar_tensor_tensor(xT[:, m, :], bk(f"{label}{m}")[:, 0:S], gate[:, m:m + 1], xT[:, m, :],
                                           ALU.mult, ALU.add).then_inc(done, 1)
                    dve.wait_ge(done, m + 1)
                    empty(dve, f"{label}{m}")

            def normed(dst, rstd, gains, root_done, done):
                dve.wait_ge(root_done, 1)
                link(V.reciprocal(rstd, rstd))
                for c in range(C):
                    V.scalar_tensor_tensor(dst[:, c, :], xT[:, c, :], gains[:, c:c + 1], rstd, ALU.mult, ALU.mult)\
                        .then_inc(done, 1)

            def gains(name):
                return cols[:, VEC[name][0]:VEC[name][0] + C]

            add_gated("y", ada[:, 2 * C:3 * C], s["xmid_set"])
            normed(hT, rstd1, amlp, s["n1_set"], s["t1_set"])
            add_gated("g", ada[:, 5 * C:6 * C], s["x1_set"])
            normed(xT, rstd2, gains("g_final"), s["n2_set"], s["xf_set"])
            dve.wait_ge(s["xf_set"], C)
            normed(hT, rstd2, gains("norm1_g_2"), s["n3_set"], s["h2_set"])

            dve.wait_ge(s["upz_set"], 1)
            for m in range(CT):
                wait_filled(dve, f"ca{m}")
                dve.wait_ge(s["sgb_set"], m + 1)
                V.tensor_tensor(up[:, m, PAD:PAD + S], bk(f"ca{m}")[:, 0:S], sgb[:, m % 2, :], ALU.mult)\
                    .then_inc(s["up_set"], 1)
                dve.wait_ge(s["up_set"], m + 1)
                empty(dve, f"ca{m}")
            n_conv = 0
            for k in range(TAPS):
                for m in range(CT):
                    src = up[:, m, k:k + S]
                    tap = cw[:, m * TAPS + k:m * TAPS + k + 1]
                    dst = mix2[:, 4 + m, :]
                    if k == 0:
                        ins = V.tensor_scalar(dst, src, tap, vcol("conv_dw_b_2", m), ALU.mult, ALU.add)
                    else:
                        dve.wait_ge(s["conv_set"], n_conv - CT + 1)
                        ins = V.scalar_tensor_tensor(dst, src, tap, dst, ALU.mult, ALU.add)
                    ins.then_inc(s["conv_set"], 1)
                    n_conv += 1
            dve.wait_ge(s["rs16_set"], 1)
            V.reciprocal(rs16, rs16).then_inc(s["rs16i_set"], 1)
            dve.wait_ge(s["consts2_in"], 32)
            dve.wait_ge(s["qk_set"], 8)
            for p in range(4):
                wait_filled(dve, f"bc{p}")
                g = vcol("q_norm_g_2" if p < 2 else "k_norm_g_2", 0)
                pair = flat(qk[:, 2 * p:2 * p + 2, :])
                V.scalar_tensor_tensor(pair, pair, g, bk(f"bc{p}"), ALU.mult, ALU.mult).then_inc(s["qn_set"], 1)
                dve.wait_ge(s["qn_set"], p + 1)
                empty(dve, f"bc{p}")
                wait_filled(dve, f"rt{p}")
                V.tensor_tensor(qt[:, p % 2, :], bk(f"rt{p}"), sin2, ALU.mult).then_inc(s["rt_set"], 1)
                link(V.tensor_tensor(pair, pair, cos2, ALU.mult))
                dve.wait_ge(s["rt_set"], p + 1)
                empty(dve, f"rt{p}")
                V.tensor_tensor(pair, pair, qt[:, p % 2, :], ALU.add).then_inc(s["qf_set"], 1)
            wait_filled(dve, "cm")
            link(V.tensor_scalar(lnr, bk("cm")[:, 0:S], 1.0 / CW, None, ALU.mult))
            empty(dve, "cm")
            for m in range(CT):
                V.tensor_tensor(mix2[:, 4 + m, :], mix2[:, 4 + m, :], lnr, ALU.subtract).then_inc(s["cmean_set"], 1)

            dve.wait_ge(s["neg_set"], 1)
            for i in range(MH + 2):
                if i < MH:
                    b = i % 2
                    wait_filled(dve, f"tc{i}")
                    if i >= 2:
                        wait_filled(dve, f"uT{i - 2}")
                    link(V.scalar_tensor_tensor(tcb[:, b, :], bk(f"tc{i}"), HD ** -0.5, neg2, ALU.mult, ALU.add))
                    empty(dve, f"tc{i}")
                    link(V.reduce_max(mx, tcb[:, b, :].rearrange("p (st k) -> p st k", st=ST), AX.X))
                    V.tensor_scalar(mneg[:, 2 * b:2 * b + 2], mx, -1.0, None, ALU.mult).then_inc(s["tmax_set"], 1)
                if 1 <= i <= MH:
                    b = (i - 1) % 2
                    dve.wait_ge(s["texp_set"], 2 * i)
                    for st in range(ST):
                        sl = tcb[:, b, st * S:(st + 1) * S]
                        ins = V.scalar_tensor_tensor(sl, sl, 1.0, cnt2[:, st * S:(st + 1) * S], ALU.mult, ALU.mult,
                                                     accum_out=rsum[:, 2 * b + st:2 * b + st + 1])
                    link(ins)
                    link(V.reciprocal(rinv[:, 2 * b:2 * b + 2], rsum[:, 2 * b:2 * b + 2]))
                    for st in range(ST):
                        sl = tcb[:, b, st * S:(st + 1) * S]
                        ins = V.tensor_scalar(sl, sl, rinv[:, 2 * b + st:2 * b + st + 1], None, ALU.mult)
                    ins.then_inc(s["tp_set"], 1)
                if i >= 3 and i % 2 == 1:
                    p = (i - 3) // 2
                    wait_filled(dve, f"pw{p}")
                    inc_emptied(V.tensor_copy(mix2[:, p, :], bk(f"pw{p}")[:, 0:S]), f"pw{p}")
                    dve.wait_ge(emptied[PLAN[f"pw{p}"][0]], PLAN[f"pw{p}"][1] + 1)
                    dve.sem_inc(s["mixa_set"], 1)
            dve.wait_ge(s["cvar_set"], 1)
            link(V.reciprocal(lnr, lnr))
            for m in range(CT):
                link(V.scalar_tensor_tensor(mix2[:, 4 + m, :], mix2[:, 4 + m, :], vcol("conv_ln_g_2", m), lnr,
                                            ALU.mult, ALU.mult))
                V.tensor_scalar(mix2[:, 4 + m, :], mix2[:, 4 + m, :], vcol("conv_ln_b_2", m), None, ALU.add)\
                    .then_inc(s["cln_set"], 1)
            dve.wait_ge(s["cln_set"], CT)
            dve.wait_ge(s["csg_set"], 1)
            V.tensor_tensor(flat(mix2[:, 4:8, :]), flat(mix2[:, 4:8, :]), flat(csq), ALU.mult).then_inc(s["mixc_set"], 1)
            for m in range(C):
                wait_filled(dve, f"z{m}")
                V.tensor_tensor(xT[:, m, :], bk(f"z{m}")[:, 0:S], xT[:, m, :], ALU.add).then_inc(s["x2_set"], 1)
                dve.wait_ge(s["x2_set"], m + 1)
                empty(dve, f"z{m}")
            normed(hT, rstd2, gains("norm2_g_2"), s["n4_set"], s["h3_set"])

            wait_filled(dve, "lg")
            link(V.reduce_max(rmx, bk("lg")[:, 0:2 * NE].rearrange("p (st e) -> p st e", st=ST), AX.X))
            for st in range(ST):
                ins = V.tensor_scalar(aff[:, st, :], bk("lg")[:, st * NE:(st + 1) * NE], rmx[:, st:st + 1], None,
                                      ALU.subtract)
            link(ins)
            empty(dve, "lg")
            dve.sem_inc(s["lg_set"], 1)
            dve.wait_ge(s["lge_set"], 1)
            link(V.reduce_sum(rsm, aff, AX.X))
            link(V.reciprocal(rsm, rsm))
            for st in range(ST):
                ins = V.tensor_scalar(aff[:, st, :], aff[:, st, :], rsm[:, st:st + 1], None, ALU.mult)
            ins.then_inc(s["aff_set"], 1)
            dve.wait_ge(s["aff_set"], 1)
            dve.wait_ge(s["consts3_in"], 16)
            for i in range(8):
                wait_filled(dve, f"af{i}")
                for k in range(2):
                    e = 2 * i + k
                    for st in range(ST):
                        row = bk(f"af{i}")[:, k * S:(k + 1) * S]
                        a = aff[:, st, e:e + 1]
                        o = (k * 2 + st) * 2 * S
                        V.tensor_scalar(junk[:, o:o + S], row, a, None, ALU.is_gt, ALU.add, accum_out=rank[:, st, e:e + 1])
                        ins = V.scalar_tensor_tensor(junk[:, o + S:o + 2 * S], row, a, lower[:, st, :], ALU.is_equal, ALU.mult,
                                                     accum_out=rank2[:, st, e:e + 1])
                link(ins)
                empty(dve, f"af{i}")
            link(V.tensor_tensor(flat(rank), flat(rank), flat(rank2), ALU.add))
            for st in range(ST):
                ins = V.tensor_tensor(pick[:, st, :].rearrange("p (e t) -> p e t", e=NE),
                                      iota.unsqueeze(1).broadcast_to([P, NE, CAP]),
                                      rank[:, st, :].unsqueeze(2).broadcast_to([P, NE, CAP]), ALU.is_equal)
            ins.then_inc(s["rank_set"], 1)
            dve.wait_ge(s["rank_set"], 1)
            dve.sem_inc(s["pick_set"], 1)
            dve.wait_ge(s["yinit_set"], 8)

            dve.sem_inc(s["he_set"], 1)
            dve.sem_inc(s["sc_used"], 1)
            with dve.Fori(0, NE) as e:
                dve.wait_ge(s["sg_set"], e + 1)
                V.tensor_tensor(he.rearrange("p (a b) -> p a b", a=2), sge.rearrange("p (a b) -> p a b", a=2),
                                ps[:, 0:2, 0:FH], ALU.mult).then_inc(s["he_set"], 1)
                dve.wait_ge(s["h3_full"], e + 1)
                dve.wait_ge(s["he_set"], 2 * e + 2)
                V.tensor_tensor(he.rearrange("p (a b) -> p a b", a=2), he.rearrange("p (a b) -> p a b", a=2),
                                ps[:, 2:4, 0:FH], ALU.mult).then_inc(s["he_set"], 1)
                dve.wait_ge(s["he_set"], 2 * e + 3)
                V.transpose(hTe, he.rearrange("p (q r) -> p r q", r=FR)).then_inc(s["hTe_set"], 1)
                for j in range(4):
                    dve.wait_ge(s["sc_full"], 4 * e + j + 2)
                    V.tensor_tensor(yacc[:, :, j * DG:(j + 1) * DG], yacc[:, :, j * DG:(j + 1) * DG],
                                    ps[:, 5 + j % 2, :].rearrange("p (st n) -> p st n", st=ST), ALU.add)\
                        .then_inc(s["sc_used"], 1)
            dve.wait_ge(s["sc_used"], 1 + 4 * NE)
            dve.sem_inc(s["y_done"], 4)

        @block.tensor
        def _(pe):
            def mm(o, w, x, first, last):
                return pe.matmul(o, w, x, start=first, stop=last)

            pe.wait_ge(s["ident_in"], 16)
            pe.wait_ge(s["vecs_in"], 16 * (len(VEC) + 2))
            inc_filled(pe.transpose(bk("vec")[:, 0:NVEC], stage, ident[0:NVEC, 0:NVEC]), "vec")
            pe.wait_ge(s["cw_in"], 16)
            for m in range(CT):
                ins = pe.transpose(bk("cw")[:, m * P:m * P + TAPS], cwst[:, m * P:(m + 1) * P], ident[0:TAPS, 0:TAPS])
            inc_filled(ins, "cw")
            pe.wait_ge(s["early_in"], 48)
            inc_filled(mm(bk("rel")[0:MH, 0:384], relst, onehot, True, True), "rel")

            def turn(label, src_of):
                wait_emptied(pe, label)
                for k in range(2):
                    for st in range(ST):
                        ins = pe.transpose(bk(label)[:, (2 * k + st) * P:(2 * k + st + 1) * P], src_of(k, st),
                                           ident[:, :])
                inc_filled(ins, label)

            pe.wait_ge(s["x_in"], 16)
            for i in range(4):
                turn(f"xr{i}", lambda k, st: xnat[:, st, (2 * i + k) * P:(2 * i + k + 1) * P])
            pe.wait_ge(s["xr_set"], ST)
            for i in range(4):
                turn(f"xn{i}", lambda k, st: xn[:, st, (2 * i + k) * P:(2 * i + k + 1) * P])

            def ada_part(k, ms):
                w = unit_ap(f"ada{k}", C, D)
                for m in ms:
                    for c in range(C):
                        ins = mm(bk(f"ada{k}")[:, m:m + 1], w[:, c, m * P:(m + 1) * P], cact[:, c:c + 1],
                                 c == 0, c == C - 1)
                return ins

            def used(ins):
                ins.then_inc(s["unit_used"], 1)

            def bank_done(label):
                pe.sem_inc(filled[PLAN[label][0]], 1)

            pe.wait_ge(s["adacol_set"], 1)
            n_used = [0]

            def finish(label, ins):
                used(ins)
                n_used[0] += 1
                pe.wait_ge(s["unit_used"], n_used[0])
                bank_done(label)

            for k in range(2):
                wait_unit(pe, f"ada{k}")
                wait_emptied(pe, f"ada{k}")
                finish(f"ada{k}", ada_part(k, range(C)))

            def proj(label, w, m0, x, wait=None, n=P, k=C, last=False, after=None):
                wait_emptied(pe, label)
                for c in range(k):
                    if wait is not None:
                        pe.wait_ge(wait, c + 1)
                    ins = mm(bk(label)[0:n, 0:S], w[:, c, m0:m0 + n], x[:, c, :], c == 0, c == k - 1)
                if last:
                    finish(label, ins)
                else:
                    inc_filled(ins, label)

            def proj_rows(label, w, c0, x, st, last=False):
                wait_emptied(pe, label)
                for c in range(C):
                    ins = mm(bk(label), x[:, c, st * P:(st + 1) * P], w[:, c, c0:c0 + 512], c == 0, c == C - 1)
                if last:
                    finish(label, ins)
                else:
                    inc_filled(ins, label)

            wait_unit(pe, "win_a")
            pe.wait_ge(unit_in2, 16)
            w = unit_ap("win_a", C, 512)
            o = (UNIT["win_a"] % 3) * BLOCK + C * 512
            wg = ring[:, o:o + C * RANK].rearrange("p (c n) -> p c n", c=C)
            proj("gg", wg, 0, hT, s["hT_set"], n=RANK)
            proj("gq0", w, 0, hT)
            proj("gq1", w, P, hT)
            proj("gk0", w, 2 * P, hT)
            proj("gk1", w, 3 * P, hT, last=True)
            pe.wait_ge(s["ggT_set"], 1)
            pe.wait_ge(s["small_in"], 32)
            wait_emptied(pe, "z")
            for mt in range(2):
                ins = mm(bk("z")[:, mt * S:(mt + 1) * S], wgate[:, mt * P:(mt + 1) * P], ggT, True, True)
            inc_filled(ins, "z")
            pe.wait_ge(s["relW_in"], 16)
            for i in range(4):
                wait_emptied(pe, f"wf{i}")
                inc_filled(mm(bk(f"wf{i}"), flip, flat(relR[:, 2 * i:2 * i + 2, :]), True, True), f"wf{i}")
            wait_unit(pe, "win_b")
            w = unit_ap("win_b", C, 1024)
            for st in range(ST):
                proj_rows(f"gv{st}", w, 0, hT, st)
            for h in range(GH):
                proj(f"gr{h}", w, 512 + h * P, hT, last=(h == GH - 1))
            wait_unit(pe, "win_c")
            w = unit_ap("win_c", C, 1024)
            for m in range(4):
                proj(f"mq{m}", w, m * P, hT)
            for m in range(4):
                proj(f"mk{m}", w, 512 + m * P, hT, last=(m == 3))
            pe.wait_ge(s["gla_set"], 6)
            turn("klT", lambda k, st: kl[:, k * S + st * P:k * S + (st + 1) * P])
            for par in range(2):
                hp = GDK * par
                wait_emptied(pe, f"att{par}")
                for k in range(2):
                    for n in range(NCH):
                        np_ = CH * (n % 2)
                        t0 = k * S + n * CH
                        o0 = (k * 2 + n // 2) * CH
                        ins = mm(bk(f"att{par}")[np_:np_ + CH, o0:o0 + CH], ke[hp:hp + GDK, t0:t0 + CH],
                                 qe[hp:hp + GDK, t0:t0 + CH], True, True)
                inc_filled(ins, f"att{par}")
            pe.wait_ge(s["klnat_set"], 1)
            pe.wait_ge(s["gv_set"], 2)
            for label, chunks in (("kv0", (0, 2)), ("kv1", (1,))):
                wait_emptied(pe, label)
                for n in chunks:
                    for h in range(GH):
                        hp, np_ = GDK * (h % 2), CH * (n % 2)
                        k0 = ((h // 2) * 2 + n // 2) * P + hp
                        o0 = ((n // 2) * 2 + h // 2) * GDV
                        ins = mm(bk(label)[hp:hp + GDK, o0:o0 + GDV], klnat[np_:np_ + CH, k0:k0 + GDK],
                                 gv[np_:np_ + CH, n // 2, h * GDV:(h + 1) * GDV], True, True)
                inc_filled(ins, label)
            wait_unit(pe, "win_d")
            w = unit_ap("win_d", C, 512)
            for st in range(ST):
                proj_rows(f"mv{st}", w, 0, hT, st, last=(st == 1))
            pe.wait_ge(s["att_set"], GH)
            pe.wait_ge(s["S_set"], 1)
            for h in range(GH):
                label = f"o{h // 2}"
                if h % 2 == 0:
                    wait_emptied(pe, label)
                o_ap = bk(label)[:, (h % 2) * S:(h % 2) * S + S]
                for pair in range(2):
                    mm(o_ap[:, pair * P:(pair + 1) * P], gv[:, pair, h * GDV:(h + 1) * GDV], att[:, h, pair, :],
                       True, False)
                    for n in range(max(1, 2 * pair), 2 * pair + 2):
                        t0 = (h // 2) * S + n * CH
                        ins = mm(o_ap[:, n * CH:(n + 1) * CH], S_at(Sst, n - 1, h // 2),
                                 (qb, qb1)[h % 2][:, t0:t0 + CH], False, n % 2 == 1)
                if h % 2:
                    inc_filled(ins, label)
            pe.wait_ge(s["ones_set"], 1)
            for i in range(2):
                pe.wait_ge(s["osq_set"], i + 1)
                wait_emptied(pe, f"gs{i}")
                inc_filled(mm(bk(f"gs{i}"), ones[:, :], osq[:, i * 512:(i + 1) * 512], True, True), f"gs{i}")

            pe.wait_ge(s["mqk_set"], 8)
            for i in range(MH + 2):
                if i < MH:
                    hp, mt = 64 * (i % 2), i // 2
                    wait_emptied(pe, f"sc{i}")
                    mm(bk(f"sc{i}")[:, 0:P], mq[hp:hp + HD, mt, 0:P], mk[hp:hp + HD, mt, 0:P], True, True)
                    inc_filled(mm(bk(f"sc{i}")[:, P:P + S], mq[hp:hp + HD, mt, P:2 * P], mk[hp:hp + HD, mt, :],
                                  True, True), f"sc{i}")
                    k = 2 + i // 2
                    if i % 2 == 0:
                        wait_unit(pe, f"ada{k}")
                        wait_emptied(pe, f"ada{k}")
                        finish(f"ada{k}", ada_part(k, range(C)))
                if 1 <= i <= MH:
                    j = i - 1
                    b = j % 2
                    pe.wait_ge(s["p_set"], j + 1)
                    wait_emptied(pe, f"pT{j}")
                    pe.transpose(bk(f"pT{j}")[:, 0:P], scb[:, b, 0:P], ident[:, :])
                    pe.transpose(bk(f"pT{j}")[:, P:2 * P], scb[:, b, P:2 * P], ident[:, :])
                    inc_filled(pe.transpose(bk(f"pT{j}")[:, 2 * P:3 * P], scb[:, b, 2 * P:3 * P], ident[:, :]),
                               f"pT{j}")
                if i >= 2:
                    j = i - 2
                    hp = 64 * (j % 2)
                    label = f"pv{j // 2}"
                    if j % 2 == 0:
                        wait_emptied(pe, label)
                    pe.wait_ge(s["pT_set"], j + 1)
                    pe.wait_ge(s["mv_set"], 2)
                    pt = pTb[:, j % 2, :]
                    mm(bk(label)[hp:hp + HD, 0:S], mv[:, 0, j * HD:(j + 1) * HD], pt[:, 0:S], True, False)
                    ins = mm(bk(label)[hp:hp + HD, P:S], mv[:, 1, j * HD:(j + 1) * HD], pt[:, S:384], False, True)
                    if j % 2:
                        inc_filled(ins, label)

            def out_proj(y, n_label, w_of, x, ready, sq, sq_done, units):
                def square_sum(c):
                    if c == 0:
                        wait_emptied(pe, n_label)
                    pe.wait_ge(sq_done, c + 1)
                    ins = mm(bk(n_label)[:, 0:S], ones[:, :], sq[:, c, :], c == 0, c == C - 1)
                    if c == C - 1:
                        inc_filled(ins, n_label)

                for m in range(C):
                    w, m0, last = w_of(m)
                    if m == 0:
                        ready()
                    if m in units:
                        wait_unit(pe, units[m])
                    proj(f"{y}{m}", w, m0, x, last=last)
                    if m >= 2:
                        square_sum(m - 2)
                square_sum(C - 2)
                square_sum(C - 1)

            def mixed():
                pe.wait_ge(s["mixg_set"], GH)
                pe.wait_ge(s["mixm_set"], 4)

            w = unit_ap("wout", C, D)
            out_proj("y", "n_mlp", lambda m: (w, m * P, m == C - 1), mix, mixed, sq1, s["sq1_set"], {0: "wout"})
            for u in range(4):
                wait_unit(pe, f"ff1_{u}")
                w = unit_ap(f"ff1_{u}", C, D)
                for m in range(C):
                    proj(f"f{C * u + m}", w, m * P, hT, s["h_set"] if u == 0 and m == 0 else None, last=(m == C - 1))
            for u in range(4):
                wait_unit(pe, f"ff2_{u}")
                w = unit_ap(f"ff2_{u}", C, D)
                for m in range(C):
                    if u == 0:
                        wait_emptied(pe, f"g{m}")
                    if u == 0 and m == 0:
                        for b in range(8):
                            pe.wait_ge(emptied[b], PLAN[f"g{b}"][1])
                    for c in range(C):
                        ins = mm(bk(f"g{m}")[:, 0:S], w[:, c, m * P:(m + 1) * P], h1[:, C * u + c, :],
                                 u == 0 and c == 0, u == 3 and c == C - 1)
                    if m == C - 1:
                        used(ins)
                        n_used[0] += 1
                    if u == 3 and m < C - 1:
                        inc_filled(ins, f"g{m}")
            pe.wait_ge(s["unit_used"], n_used[0])
            bank_done("g7")
            pe.sem_inc(s["hid_used"], 1)

            def norm_sum(label, sq, done):
                wait_emptied(pe, label)
                for c in range(C):
                    pe.wait_ge(done, c + 1)
                    ins = mm(bk(label)[:, 0:S], ones[:, :], sq[:, c, :], c == 0, c == C - 1)
                inc_filled(ins, label)

            norm_sum("n_fin", sq2, s["sq2_set"])
            norm_sum("n_one", sq2, s["sqf_set"])

            wait_unit(pe, "conv")
            w = unit_ap("conv", C, 1024)
            for m in range(CT):
                proj(f"cb{m}", w, CW + m * P, hT, s["h2_set"] if m == 0 else None)
                proj(f"ca{m}", w, m * P, hT, last=(m == CT - 1))
            wait_unit(pe, "qk")
            w = unit_ap("qk", C, 1024)
            pe.wait_ge(s["consts2_in"], 32)

            def q_squares(m):
                if m == 0:
                    wait_emptied(pe, "qs")
                pe.wait_ge(s["qsq_set"], m + 1)
                mm(bk("qs")[0:16, 0:S], selh[:, 16 * m:16 * m + 16], qsq[:, m % 2, :], m == 0, m == 7)\
                    .then_inc(s["pe_link"], 1)

            for m in range(8):
                proj(f"qk{m}", w, m * P, hT, last=(m == 7))
                if m >= 1:
                    q_squares(m - 1)
            q_squares(7)
            pe.wait_ge(s["pe_link"], 8)
            bank_done("qs")
            wait_unit(pe, "v")
            w = unit_ap("v", C, 512)
            for st in range(ST):
                proj_rows(f"v{st}", w, 0, hT, st, last=(st == 1))
            pe.wait_ge(s["rs16i_set"], 1)
            for p in range(4):
                wait_emptied(pe, f"bc{p}")
                for k in range(2):
                    m = 2 * p + k
                    ins = mm(bk(f"bc{p}")[:, k * S:(k + 1) * S], bsel[:, m * P:(m + 1) * P], rs16, True, True)
                inc_filled(ins, f"bc{p}")
                pe.wait_ge(s["qn_set"], p + 1)
                wait_emptied(pe, f"rt{p}")
                inc_filled(mm(bk(f"rt{p}"), rot, flat(qk[:, 2 * p:2 * p + 2, :]), True, True), f"rt{p}")
            pe.wait_ge(s["conv_set"], TAPS * CT)
            wait_emptied(pe, "cm")
            for m in range(CT):
                ins = mm(bk("cm")[:, 0:S], ones[:, :], mix2[:, 4 + m, :], m == 0, m == CT - 1)
            inc_filled(ins, "cm")
            pe.wait_ge(s["qf_set"], 4)
            pe.wait_ge(s["v_set"], 2)
            for i in range(MH + 2):
                if i < MH:
                    hp, mt = 64 * (i % 2), i // 2
                    wait_emptied(pe, f"tc{i}")
                    for st in range(ST):
                        ins = mm(bk(f"tc{i}")[:, st * S:(st + 1) * S], qk[hp:hp + HD, mt, st * P:(st + 1) * P],
                                 qk[hp:hp + HD, 4 + mt, :], True, True)
                    inc_filled(ins, f"tc{i}")
                if 1 <= i <= MH:
                    j = i - 1
                    b = j % 2
                    pe.wait_ge(s["tp_set"], j + 1)
                    wait_emptied(pe, f"uT{j}")
                    for kt in range(ST):
                        for st in range(ST):
                            ins = pe.transpose(bk(f"uT{j}")[:, kt * S + st * P:kt * S + (st + 1) * P],
                                               tcb[:, b, st * S + kt * P:st * S + (kt + 1) * P], ident[:, :])
                    inc_filled(ins, f"uT{j}")
                if i >= 2:
                    j = i - 2
                    hp = 64 * (j % 2)
                    label = f"pw{j // 2}"
                    if j % 2 == 0:
                        wait_emptied(pe, label)
                    pe.wait_ge(s["uT_set"], j + 1)
                    for kt in range(ST):
                        ins = mm(bk(label)[hp:hp + HD, 0:S], vn[:, kt, j * HD:(j + 1) * HD],
                                 uTb[:, j % 2, kt * S:(kt + 1) * S], kt == 0, kt == 1)
                    if j % 2:
                        inc_filled(ins, label)
            pe.wait_ge(s["csq_set"], 1)
            wait_emptied(pe, "cv")
            for m in range(CT):
                ins = mm(bk("cv")[:, 0:S], ones[:, :], csq[:, m, :], m == 0, m == CT - 1)
            inc_filled(ins, "cv")

            def mixed2():
                pe.wait_ge(s["mixa_set"], 4)
                pe.wait_ge(s["mixc_set"], 1)

            w0, w1_ = unit_ap("wo2_0", C, 512), unit_ap("wo2_1", C, 512)
            out_proj("z", "n_two", lambda m: ((w0, w1_)[m // 4], (m % 4) * P, m % 4 == 3), mix2, mixed2,
                     sq2, s["sq3_set"], {0: "wo2_0", 4: "wo2_1"})
            wait_emptied(pe, "lg")
            pe.wait_ge(s["h3_set"], C)
            for st in range(ST):
                for c in range(C):
                    ins = mm(bk("lg")[:, st * NE:(st + 1) * NE], hT[:, c, st * P:(st + 1) * P],
                             wr[:, c * NE:(c + 1) * NE], c == 0, c == C - 1)
            inc_filled(ins, "lg")
            for i in range(4):
                turn(f"hn{i}", lambda k, st: hT[:, 2 * i + k, st * P:(st + 1) * P])
            for i in range(4):
                turn(f"xf{i}", lambda k, st: xT[:, 2 * i + k, st * P:(st + 1) * P])
            pe.wait_ge(s["aff_set"], 1)
            for i in range(8):
                wait_emptied(pe, f"af{i}")
                for k in range(2):
                    for st in range(ST):
                        ins = pe.transpose(bk(f"af{i}")[:, k * S + st * P:k * S + (st + 1) * P],
                                           aff[:, st, 2 * i + k:2 * i + k + 1].broadcast_to([P, P]), ident[:, :])
                inc_filled(ins, f"af{i}")
            pe.wait_ge(s["pick_set"], 1)
            pe.wait_ge(s["hnat_set"], 8)
            for b in range(8):
                n = max(u + 1 for bb_, u in PLAN.values() if bb_ == b)
                pe.wait_ge(emptied[b], n)

            pe.sem_inc(s["pgT_full"], 1)
            pe.sem_inc(s["sc_full"], 1)
            with pe.Fori(0, NE) as e:
                pe.wait_ge(s["xe_set"], 1 + e)
                for c in range(C):
                    for st in range(ST):
                        ins = mm(ps[:, 7, c * CAP:(c + 1) * CAP],
                                 hnat[:, st, c * P:(c + 1) * P],
                                 pick[:, st, bass.ds(e * CAP, CAP)], st == 0, st == 1)
                ins.then_inc(s["xe_full"], 1)
                pe.wait_ge(s["pgs_set"], e + 1)
                pe.wait_ge(s["ye_set"], 1 + e)
                for st in range(ST):
                    ins = pe.transpose(ps[:, 4, st * P:(st + 1) * P], pgs[:, st, :], ident[:, :])
                ins.then_inc(s["pgT_full"], 1)
                pe.wait_ge(s["xe_set"], e + 2)
                for mat, (full, bank) in enumerate(((s["h1_full"], 0), (s["h3_full"], 2))):
                    pe.wait_ge(s["he_set"], 1 + 2 * e)
                    for c in range(C):
                        q = mat * C + c
                        slot = (9 + q) % NSLOT
                        pe.wait_ge(chunk_in[slot], 32 * e + 16 * (q // NSLOT + 1))
                        w = ring[:, slot * SLOT:(slot + 1) * SLOT]
                        for half in range(2):
                            for j in range(4):
                                c0 = j * FG + half * FH
                                ins = mm(ps[32 * j:32 * j + CAP, bank + half, 0:FH], xe[:, c, :], w[:, c0:c0 + FH],
                                         c == 0, c == C - 1)
                        ins.then_inc(s["w_used"], 1)
                    pe.wait_ge(s["w_used"], NCHUNK * e + (mat + 1) * C)
                    pe.sem_inc(full, 1)
                pe.wait_ge(s["hTe_set"], e + 1)
                pe.wait_ge(s["pgT_set"], e + 1)
                w2v = ring[:, 1 * SLOT:9 * SLOT].rearrange("p (r n) -> p r n", r=FR)
                got = 0
                for r in range(FR):
                    while got * SLOT < (r + 1) * D:
                        q = 2 * C + got
                        slot = (9 + q) % NSLOT
                        pe.wait_ge(chunk_in[slot], 32 * e + 16 * (q // NSLOT + 1))
                        got += 1
                    for j in range(4):
                        ins = mm(ps[32 * j:32 * j + CAP, 4, 0:DG], hTe[:, r, :], w2v[:, r, j * DG:(j + 1) * DG],
                                 r == 0, r == FR - 1)
                    if any((k * SLOT - 1) // D == r for k in range(1, C + 1)):
                        ins.then_inc(s["w_used"], 1)
                pe.wait_ge(s["w_used"], NCHUNK * e + NCHUNK)
                pe.sem_inc(s["ye_full"], 1)
                pe.wait_ge(s["ye_set"], e + 2)
                pe.wait_ge(s["pgT_set"], e + 1)
                for j in range(4):
                    if j < 2:
                        pe.wait_ge(s["sc_used"], 1 + 4 * e)
                    else:
                        pe.wait_ge(s["sc_used"], 4 * e + j)
                    for st in range(ST):
                        ins = mm(ps[:, 5 + j % 2, st * DG:(st + 1) * DG], pgT[32 * j:32 * j + CAP, st * P:(st + 1) * P],
                                 ye[32 * j:32 * j + CAP, :], True, True)
                    ins.then_inc(s["sc_full"], 1)


def S_at(Sst, n, mt):
    return Sst[:, n, mt, :]


def tables():
    f = np.float32
    p = np.arange(P)
    n = np.arange(S)
    ratio = np.maximum(n, 1).astype(f) / f(16)
    large = 16 + (np.log(ratio) / f(np.log(8.0)) * f(16)).astype(np.int32)
    bucket = np.where(n < 16, n, np.minimum(large, BUCKETS - 1))
    t1 = np.zeros((P, P + 384 + P), f)
    t1[:, P + 384:] = np.eye(P)[::-1]
    t1[:, 0:P] = np.eye(P)
    dist = S - 1 - np.arange(S)
    t1[bucket[dist], P + np.arange(S)] = 1.0
    half = HD // 2
    inv = (f(10000.0) ** (-np.arange(half, dtype=f) / f(half))).astype(f)
    ang = (np.arange(S, dtype=f)[:, None] * inv[None, :]).astype(f)
    cos, sin = np.cos(ang).T, np.sin(ang).T
    t2 = np.zeros((P, 2816), f)
    t2[:, 0:512] = np.tile(cos, (4, 2))
    t2[:, 512:1024] = np.tile(sin, (4, 2))
    q = (np.arange(ST)[None, :, None] * P + p[:, None, None])
    diff = q - np.arange(S)[None, None, :]
    count = (abs(diff) <= 64).astype(f) + (diff % 4 == 0) + (diff % 16 == 0)
    t2[:, 1024:1536] = count.reshape(P, 512)
    for i in range(P):
        if i % HD < half:
            t2[i + half, 1536 + i] = -1.0
        else:
            t2[i - half, 1536 + i] = 1.0
    for m in range(8):
        for i in range(P):
            t2[i, 1664 + 16 * m + 2 * m + i // HD] = 1.0
            t2[2 * m + i // HD, 1792 + m * P + i] = 1.0
    t3 = np.zeros((P, 512 + CAP), f)
    t3[:, 0:512] = (np.arange(S)[None, None, :] < q).reshape(P, 512)
    t3[:, 512:] = np.arange(CAP)
    return {"table1": t1, "table2": t2, "table3": t3}


_INS = ["x", "c", "w_ada", "b_ada", "g_mix", "w_in", "w_gla_gate", "b_gla_gate", "g_gla_out", "rel_bias", "w_out",
        "g_mlp", "w_ff1", "w_ff2", "g_final", "norm1_g_2", "w_in_2", "q_norm_g_2", "k_norm_g_2", "conv_dw_w_2",
        "conv_dw_b_2", "conv_ln_g_2", "conv_ln_b_2", "w_out_2", "norm2_g_2", "w_router_2", "w1_2", "w3_2", "w2_2"]
_LAYERED = ("w_ada", "w_in", "w_gla_gate", "w_out", "w_ff1", "w_ff2")


def kernel(**inputs):
    import concourse.bacc as bacc
    from concourse.bass_utils import run_bass_kernel_spmd

    nc = bacc.Bacc("TRN2", target_bir_lowering=False, num_devices=1)
    arrays, args = {}, {}
    given = {name: np.ascontiguousarray(inputs[name]) for name in _INS}
    given.update(tables())
    for name, a in given.items():
        arrays[f"in_{name}"] = a
        ap = nc.dram_tensor(f"in_{name}", a.shape, mybir.dt.from_np(a.dtype), kind="ExternalInput").ap()
        args[name] = ap[0] if name in _LAYERED else ap
    out = nc.dram_tensor("out_0", (1, S, D), F32, kind="ExternalOutput").ap()
    rel_dram = nc.dram_tensor("rel_rows", (MH, 384), F32, kind="Internal").ap()
    build(nc, args, out, rel_dram)
    r = run_bass_kernel_spmd(nc, [arrays], core_ids=[0])
    return r.results[0]["out_0"]
```

```python
from contextlib import ExitStack

import numpy as np
import concourse.bass as bass
from concourse import mybir

F32 = mybir.dt.float32
ALU = mybir.AluOpType
ACT = mybir.ActivationFunctionType
AX = mybir.AxisListType

P = 128
D = 1024
S = 256
ST = S // P
C = D // P
EPS = 1e-6
NEG = -1e30
GH, GDV, GDK, RANK, CH = 4, 128, 64, 16, 64
NCH = S // CH
QKW, VW = GH * GDK, GH * GDV
MH, HD = 8, 64
MW = MH * HD
FF = 4 * D
BUCKETS = 32
TAPS = 31
PAD = TAPS // 2
CW = 512
CT = CW // P
NE, CAP, FE = 16, 32, 2816
FG = FE // 4
FH = FG // 2
FR = FE // P
DG = D // 4

SLOT = FE
NSLOT = 12
BLOCK = 3 * SLOT
NCHUNK = 24
AR = 14400

UNITS = (["ada0", "ada1", "win_a", "win_b", "win_c", "win_d", "ada2", "ada3", "ada4", "ada5", "wout"]
         + [f"ff1_{u}" for u in range(4)] + [f"ff2_{u}" for u in range(4)]
         + ["conv", "qk", "v", "wo2_0", "wo2_1"])
UNIT = {name: i for i, name in enumerate(UNITS)}
assert (len(UNITS) - 1) % 3 == 2

VEC = {}
for _name, _n in (("b_ada", 48), ("c", 8), ("g_mix", 8), ("g_mlp", 8), ("g_final", 8), ("norm1_g_2", 8),
                  ("norm2_g_2", 8), ("b_gla_gate", 2), ("g_gla_out", 4), ("conv_dw_b_2", 4),
                  ("conv_ln_g_2", 4), ("conv_ln_b_2", 4), ("q_norm_g_2", 1), ("k_norm_g_2", 1)):
    VEC[_name] = (sum(n for _, n in VEC.values()), _n)
NVEC = sum(n for _, n in VEC.values())


def bank_plan():
    order = ["rel", "n_in", "ada0", "at0", "ada1", "at1", "gg", "gq0", "gq1", "gk0", "gk1", "z"]
    order += [f"wf{i}" for i in range(4)] + ["gv0", "gv1"] + [f"gr{i}" for i in range(4)]
    order += [f"mq{i}" for i in range(4)] + [f"mk{i}" for i in range(4)]
    order += ["klT", "att0", "att1", "kv0", "kv1", "mv0", "mv1", "o0", "o1", "gs0", "gs1"]
    for i in range(MH + 2):
        order += [f"sc{j}" for j in ((0, 1) if i == 0 else (i + 1,)) if j < MH]
        if i < MH:
            order.append(f"{('ada', 'at')[i % 2]}{2 + i // 2}")
        if 1 <= i <= MH:
            order.append(f"pT{i - 1}")
        if i >= 2 and i % 2 == 0:
            order.append(f"pv{i // 2 - 1}")
    order += ["n_mlp"] + [f"y{m}" for m in range(C)] + [f"f{m}" for m in range(FF // P)]
    held = {"n_mlp": {f"y{m}" for m in range(C)}}
    order += [f"g{m}" for m in range(C)] + ["n_fin", "n_one"]
    for m in range(CT):
        order += [f"cb{m}", f"ca{m}"]
    order += ["qs"] + [f"qk{m}" for m in range(8)] + ["v0", "bc0", "bc1", "cm", "v1", "rt0"]
    order += ["bc2", "rt1", "bc3", "rt2", "rt3", "cv"]
    held["qs"] = {f"qk{m}" for m in range(8)}
    for i in range(MH + 2):
        order += [f"tc{j}" for j in ((0, 1) if i == 0 else (i + 1,)) if j < MH]
        if 1 <= i <= MH:
            order.append(f"uT{i - 1}")
        if i >= 2 and i % 2 == 0:
            order.append(f"pw{i // 2 - 1}")
    order += ["n_two"] + [f"z{m}" for m in range(C)]
    held["n_two"] = {f"z{m}" for m in range(C)}
    order += ["lg"] + [f"hn{i}" for i in range(4)] + ["aT"] + [f"xf{i}" for i in range(4)] + ["rk"]
    plan, used, nxt, kept = {}, [0] * 8, 0, {}
    for label in order:
        taken = {b for b, rest in kept.items() if label in rest}
        while nxt % 8 in taken:
            nxt += 1
        if label == "g0":
            nxt = 0
        plan[label] = (nxt % 8, used[nxt % 8])
        used[nxt % 8] += 1
        if label in held:
            kept[nxt % 8] = held[label]
        nxt += 1
    return plan


def build(nc, T, out, rel_dram):
    PLAN = bank_plan()
    with ExitStack() as ctx:
        def sb(name, cols):
            return ctx.enter_context(nc.sbuf_tensor(name, [P, cols], F32))

        def sem(name):
            return ctx.enter_context(nc.semaphore(name))

        ring = sb("ring", NSLOT * SLOT)
        arena = sb("arena", AR)
        xT_ = sb("xT", C * S)
        hT_ = sb("hT", C * S)
        ident = sb("ident", P)
        ones = sb("ones", P)
        table = sb("table", NVEC + CT * TAPS + C * NE)
        cols = table[:, 0:NVEC]
        ada = sb("ada", 48)
        cw = table[:, NVEC:NVEC + CT * TAPS]
        wr = table[:, NVEC + CT * TAPS:]
        small = sb("small", 96)
        ps = ctx.enter_context(nc.psum_tensor("ps", [P, 8, 512], F32))

        xT = xT_[:, :].rearrange("p (c s) -> p c s", c=C)
        hT = hT_[:, :].rearrange("p (c s) -> p c s", c=C)
        ext = ring[:, 9 * SLOT:12 * SLOT]

        def ar(off, words, **dims):
            ap = arena[:, off:off + words]
            if dims:
                names = list(dims)
                ap = ap.rearrange(f"p ({' '.join(names)} last) -> p {' '.join(names)} last", **dims)
            return ap

        def ex(off, words, **dims):
            ap = ext[:, off:off + words]
            if dims:
                names = list(dims)
                ap = ap.rearrange(f"p ({' '.join(names)} last) -> p {' '.join(names)} last", **dims)
            return ap

        eps = small[:, 0:1]
        spare = small[:, 1:2]
        cact = small[:, 8:16]
        amix = small[:, 16:24]
        dec = small[:, 24:32]
        mx = small[:, 32:34]
        mneg = small[:, 34:38]
        rsum = small[:, 38:42]
        rinv = small[:, 42:46]
        amlp = small[:, 48:56]
        sg8 = small[:, 56:64]

        sq0 = ar(0, 2048, c=C)
        rstd0 = ar(2048, 256)
        adarow = ar(14080, 256)
        gv = ar(0, 1024, st=ST)
        gr = ar(1024, 1024, h=GH)
        sgr = ar(2048, 1024, h=GH)
        oT = ar(3072, 1024, h=GH)
        gq, gk, zz, tt, bb, qe, ke, kl, qb = (ar(4096 + 512 * i, 512) for i in range(9))
        klnat = ar(8704, 512)
        att = ar(5120, 1024, h=GH, pair=2)
        qb1 = ar(9216, 512)
        Sst = ar(9728, 768, before=3, pair=2)
        osq = ar(10496, 1024)
        mix = ar(11520, 2048, c=C)
        ggT = arena[0:RANK, 13568:13824]
        wgate = arena[0:RANK, 13824:14080]
        scanm = ar(10496, 512)
        rso = ar(5120, 1024)
        sq1 = ar(8192, 2048, c=C)
        rstd1 = ar(10240, 256)
        h1 = ar(0, 8192, m=FF // P)
        relst = arena[0:BUCKETS, 4736:4744]
        relW = ex(0, 2048, h=MH)
        relR = ex(2048, 2048, h=MH)
        scb = ex(2048, 768, b=2)
        pTb = ex(2816, 768, b=2)
        mq = ex(3584, 1024, m=4)
        mk = ex(4608, 1024, m=4)
        mv = ex(5632, 1024, st=ST)
        flip = ex(7488, P)
        onehot = ext[0:BUCKETS, 6720:6720 + 384]
        rtb = ext[0:MH, 7104:7104 + 384]

        up = ar(0, 4 * 288, m=CT)
        sgb = ar(1152, 512, b=2)
        qk = ar(1664, 2048, m=8)
        vn = ar(3712, 1024, st=ST)
        mix2 = ar(4736, 2048, c=C)
        C2 = 6784
        cos2, sin2 = ar(C2, 512), ar(C2 + 512, 512)
        cnt2 = ar(C2 + 1024, 512)
        neg2 = ar(9600, 512)
        rot = ar(C2 + 1536, P)
        selh = ar(C2 + 1664, P)
        bsel = arena[0:16, C2 + 1792:C2 + 2816]
        sq2 = ar(10240, 2048, c=C)
        sqg = ex(0, 2048, c=C)
        gg2 = small[:, 64:72]
        rstd2 = ar(12288, 256)
        tcb = [ar(12544, 512), ar(13056, 512), ar(11264, 512)]
        uTb = ar(10240, 1024, b=2)
        qsq = ar(10240, 512, b=2)
        tapped = ar(11264, 1024, b=4)
        qt = ar(11264, 1024, b=2)
        rs16 = arena[0:16, 13568:13824]
        lnr = ar(13824, 256)
        csq = ar(0, 1024, m=CT)
        yacc = ar(0, 2048, st=ST)
        hnat = ar(2048, 2048, st=ST)
        affT, restT, equalT, aboveT, countT, placeT = (arena[0:NE, 4096 + S * i:4096 + S * (i + 1)] for i in range(6))
        top8 = arena[0:NE, 5632:5640]
        n_above = arena[0:NE, 5640:5641]
        room = arena[0:NE, 5641:5642]
        C3 = 6784
        iota = ar(C3, CAP)
        aff = ar(7400, 32, st=ST)
        place = ar(7432, 32, st=ST)
        rmx = ar(7496, 2)
        rsm = ar(7498, 2)
        pick = ar(10240, 1024, st=ST)
        xe = ar(12544, 256, c=C)
        sge = ar(4736, 704)
        he = ar(5440, 704)
        hTe = ar(7808, 704, r=FR)
        ye = ar(8512, 256)
        pgs = ar(8768, 256, st=ST)
        pgT = ar(9024, 256)

        filled = [sem(f"bank_filled{b}") for b in range(8)]
        emptied = [sem(f"bank_emptied{b}") for b in range(8)]
        unit_in = [sem(f"unit_in{b}") for b in range(3)]
        unit_in2 = sem("unit_in_gate_columns")
        chunk_in = [sem(f"chunk_in{q}") for q in range(NSLOT)]
        s = {name: sem(name) for name in """
            small_in unit_used w_used ones_set eps_set pool_link scan_set qb1z_set e_set attz_set attd_set
            att_set hid_used consts2_in upz_set neg_set tap_set conv_pool_set conv_set cm_set cmean_set crec_set
            clng_set cln_set csg_set mixc_set tp_set consts3_in pick_set pgT_full pgs_set act_link cact_set
            sq0_set n0_set rtbneg_set rel_dram_in relW_in t0_set hT_set ggT_set gqk_set z_set zl_set gv_set
            gr_set sgr_set b_set mqk_set klnat_set mv_set o_set osq_set gla_n max_set exp_set pT_set xmid_set
            sq1_set n1_set t1_set h_set relu_set x1_set sq2_set rr_set n3_set n2_set up_set sgb_set pe_link
            qsq_set qk_set rs16_set v_set tmax_set texp_set uT_set tm_set csq_set cvar_set x2_set sq3_set n4_set
            lg_set lge_set hnat_set yinit_set xe_set ye_set xe_full sc_full pgT_set h1_full he_set sg_set
            ye_full out_done dve_link adacol_set adarow_set amix_set gla_set S_set mixg_set p_set
            mixm_set h2_set xf_set rs16i_set qn_set rt_set qf_set mixa_set h3_set aff_set place_set rank_set
            sc_used h3_full hTe_set""".split()}

        def bk(label):
            return ps[:, PLAN[label][0], :]

        def wait_filled(eng, label):
            b, n = PLAN[label]
            eng.wait_ge(filled[b], n + 1)

        def wait_emptied(eng, label):
            b, n = PLAN[label]
            if n:
                eng.wait_ge(emptied[b], n)

        def inc_filled(ins, label):
            ins.then_inc(filled[PLAN[label][0]], 1)

        def inc_emptied(ins, label):
            ins.then_inc(emptied[PLAN[label][0]], 1)

        def empty(eng, label):
            eng.sem_inc(emptied[PLAN[label][0]], 1)

        def wait_unit(eng, name):
            i = UNIT[name]
            eng.wait_ge(unit_in[i % 3], 16 * (i // 3 + 1))

        def unit_ap(name, k, n):
            o = (UNIT[name] % 3) * BLOCK
            return ring[:, o:o + k * n].rearrange("p (k n) -> p k n", k=k)

        def vcol(name, i):
            return cols[:, VEC[name][0] + i:VEC[name][0] + i + 1]

        def flat(ap):
            return ap.rearrange("p a b -> p (a b)")

        block = ctx.enter_context(nc.Block())

        @block.sync
        def _(sp):
            def rows(ap, c0, n):
                return ap[:, c0:c0 + n].rearrange("(c p) n -> p c n", p=P)

            def unit_source(name):
                if name.startswith("ada"):
                    return rows(T["w_ada"], D * int(name[3]), D)
                if name.startswith("win_"):
                    c0, n = {"a": (0, 2 * QKW), "b": (512, 1024), "c": (1552, 1024), "d": (2576, 512)}[name[4]]
                    return rows(T["w_in"], c0, n)
                if name == "wout":
                    return rows(T["w_out"], 0, D)
                if name.startswith("ff1"):
                    return rows(T["w_ff1"], D * int(name[4]), D)
                if name.startswith("ff2"):
                    u = int(name[4])
                    return rows(T["w_ff2"][u * D:(u + 1) * D, :], 0, D)
                if name in ("conv", "qk", "v"):
                    c0, n = {"conv": (3 * MW, 2 * CW), "qk": (0, 2 * MW), "v": (2 * MW, MW)}[name]
                    return rows(T["w_in_2"], c0, n)
                return rows(T["w_out_2"], 512 * int(name[4]), 512)

            sp.wait_ge(s["small_in"], 16 * 8)
            for i, name in enumerate(UNITS):
                if i >= 3:
                    sp.wait_ge(s["unit_used"], i - 2)
                src = unit_source(name)
                sp.dma_start(unit_ap(name, C, src.shape[2]), src).then_inc(unit_in[i % 3], 16)
                if name == "win_a":
                    o = (i % 3) * BLOCK + C * 512
                    sp.dma_start(ring[:, o:o + C * RANK].rearrange("p (c n) -> p c n", c=C),
                                 rows(T["w_in"], 1536, RANK)).then_inc(unit_in2, 16)

            w1 = T["w1_2"].rearrange("e (c p) f -> p e c f", p=P)
            w3 = T["w3_2"].rearrange("e (c p) f -> p e c f", p=P)
            w2 = T["w2_2"].rearrange("e (p r) n -> p e (r n)", r=FR)

            def chunk(e, q):
                slot = (9 + q) % NSLOT
                if q < C:
                    src = w1[:, e, q, :]
                elif q < 2 * C:
                    src = w3[:, e, q - C, :]
                else:
                    src = w2[:, e, (q - 2 * C) * SLOT:(q - 2 * C + 1) * SLOT]
                sp.dma_start(ring[:, slot * SLOT:(slot + 1) * SLOT], src).then_inc(chunk_in[slot], 16)

            for q in range(NSLOT):
                if q == 0:
                    sp.wait_ge(s["unit_used"], UNIT["wout"] + 1)
                elif q % 3 == 0:
                    sp.wait_ge(s["unit_used"], len(UNITS) - 3 + q // 3)
                chunk(0, q)
            with sp.Fori(0, NE - 1) as e:
                for q in range(NCHUNK):
                    if q != 4:
                        sp.wait_ge(s["w_used"], NCHUNK * e + q + 1 + (q == 3))
                    if q < NSLOT:
                        chunk(e, q + NSLOT)
                    else:
                        chunk(e + 1, q - NSLOT)
            for q in range(NSLOT):
                sp.wait_ge(s["w_used"], NCHUNK * (NE - 1) + q + 1)
                chunk(NE - 1, q + NSLOT)

        @block.gpsimd
        def _(pool):
            nc.gpsimd.memset(ones[:, :], 1.0).then_inc(s["ones_set"], 1)
            nc.gpsimd.memset(eps, EPS).then_inc(s["eps_set"], 1)
            nc.gpsimd.memset(scanm, 1.0).then_inc(s["pool_link"], 1)
            pool.wait_ge(s["pool_link"], 1)
            nc.gpsimd.memset(scanm.rearrange("p (n t) -> p n t", t=CH)[:, :, 0:1], 0.0).then_inc(s["scan_set"], 1)
            nc.gpsimd.memset(qb1, 0.0).then_inc(s["qb1z_set"], 1)
            pool.wait_ge(s["e_set"], 4)
            nc.gpsimd.memset(ar(5120, 1024), 0.0).then_inc(s["attz_set"], 1)
            pool.wait_ge(s["attd_set"], 4)
            for h in range(GH):
                nc.gpsimd.affine_select(out=att[:, h, :, :], in_=att[:, h, :, :], compare_op=ALU.is_ge, fill=0.0,
                                        base=0, pattern=[[0, 2], [1, P]], channel_multiplier=-1).then_inc(s["att_set"], 1)
            pool.wait_ge(s["hid_used"], 1)
            pool.dma_start(ar(C2, 1792), T["table2"][:, 0:1792]).then_inc(s["consts2_in"], 16)
            pool.dma_start(bsel, T["table2"][0:16, 1792:2816]).then_inc(s["consts2_in"], 16)
            nc.gpsimd.memset(ar(0, 4 * 288), 0.0).then_inc(s["upz_set"], 1)
            pool.wait_ge(s["consts2_in"], 32)
            nc.gpsimd.tensor_scalar(neg2, cnt2, 0.0, NEG, ALU.is_equal, ALU.mult).then_inc(s["neg_set"], 1)
            pool.wait_ge(s["tap_set"], 1)
            for k in range(1, TAPS):
                pool.wait_ge(s["tap_set"], k + 1)
                if k >= 2:
                    pool.wait_ge(s["conv_pool_set"], k - 1)
                nc.gpsimd.tensor_tensor(mix2[:, C - 1, :], mix2[:, C - 1, :], tapped[:, k % 4, :], ALU.add)\
                    .then_inc(s["conv_pool_set"], 1)
            conv = mix2[:, 4:8, :]
            lnr4 = lnr.unsqueeze(1).broadcast_to([P, CT, S])
            pool.wait_ge(s["conv_set"], TAPS * (CT - 1))
            pool.wait_ge(s["conv_pool_set"], TAPS - 1)
            pool.wait_ge(s["cm_set"], 1)
            nc.gpsimd.tensor_tensor(conv, conv, lnr4, ALU.subtract).then_inc(s["cmean_set"], 1)
            pool.wait_ge(s["cmean_set"], 1)
            pool.wait_ge(s["crec_set"], 1)
            nc.gpsimd.tensor_tensor(conv, conv, lnr4, ALU.mult).then_inc(s["clng_set"], 1)
            pool.wait_ge(s["clng_set"], 1)
            for m in range(CT):
                nc.gpsimd.tensor_scalar(mix2[:, 4 + m, :], mix2[:, 4 + m, :], vcol("conv_ln_g_2", m),
                                        vcol("conv_ln_b_2", m), ALU.mult, ALU.add).then_inc(s["cln_set"], 1)
            pool.wait_ge(s["cln_set"], CT)
            pool.wait_ge(s["csg_set"], 1)
            nc.gpsimd.tensor_tensor(conv, conv, csq, ALU.mult).then_inc(s["mixc_set"], 1)
            pool.wait_ge(s["tp_set"], 2 * MH)
            pool.dma_start(iota, T["table3"]).then_inc(s["consts3_in"], 16)

            pool.wait_ge(s["pick_set"], 1)
            with pool.Fori(0, NE) as e:
                pool.wait_ge(s["pgT_full"], 1 + e)
                for st in range(ST):
                    ins = nc.gpsimd.tensor_tensor(
                        pgs[:, st, :].rearrange("p (j t) -> p j t", j=4),
                        pick[:, st, bass.ds(e * CAP, CAP)].unsqueeze(1).broadcast_to([P, 4, CAP]),
                        aff[:, st, bass.ds(e, 1)].unsqueeze(1).broadcast_to([P, 4, CAP]), ALU.mult)
                ins.then_inc(s["pgs_set"], 1)

        @block.scalar
        def _(act):
            n_link = [0]

            def link(ins):
                n_link[0] += 1
                ins.then_inc(s["act_link"], 1)
                act.wait_ge(s["act_link"], n_link[0])

            A = nc.scalar.activation
            for dst, src in ((xT_[:, :].rearrange("p (c s) -> p c s", c=C), T["x_turned"]), (table[:, :], T["table0"]),
                             (relst, T["rel_bias"]), (onehot, T["table1"][0:BUCKETS, P:P + 384]),
                             (ident[:, :], T["table1"][:, 0:P]), (flip, T["table1"][:, P + 384:]),
                             (wgate, T["w_gla_gate"])):
                act.dma_start(dst, src).then_inc(s["small_in"], 16)
            act.sem_inc(s["small_in"], 16)
            act.wait_ge(s["eps_set"], 1)
            act.wait_ge(s["small_in"], 16 * 8)

            def squares(ready, dst, n0, done):
                for c in range(C):
                    if ready is not None:
                        act.wait_ge(ready, n0 + c + 1)
                    A(dst[:, c, :], xT[:, c, :], ACT.Square).then_inc(done, 1)

            def root(label, dst, done):
                wait_filled(act, label)
                A(dst, bk(label)[:, 0:S], ACT.Sqrt, bias=eps, scale=1.0 / D).then_inc(done, 1)
                act.wait_ge(done, 1)
                empty(act, label)

            A(sg8, cols[:, VEC["c"][0]:VEC["c"][0] + C], ACT.Sigmoid).then_inc(s["cact_set"], 1)
            squares(None, sq0, 0, s["sq0_set"])
            root("n_in", rstd0, s["n0_set"])
            wait_filled(act, "rel")
            inc_emptied(A(rtb[:, 0:S], bk("rel")[0:MH, 0:S], ACT.Copy), "rel")
            act.wait_ge(emptied[PLAN["rel"][0]], PLAN["rel"][1] + 1)
            act.wait_ge(s["rtbneg_set"], 1)
            act.dma_start(rel_dram, rtb).then_inc(s["rel_dram_in"], 16)
            act.wait_ge(s["rel_dram_in"], 16)
            act.dma_start(relR, bass.AP(rel_dram.tensor, 0, [[1, P], [384, MH], [1, S]])).then_inc(s["relW_in"], 16)

            for c in range(C):
                act.wait_ge(s["t0_set"], c + 1)
                A(hT[:, c, :], hT[:, c, :], ACT.Identity, bias=ada[:, c:c + 1]).then_inc(s["hT_set"], 1)

            def evac(label, dst, src, done, func=ACT.Copy, **kw):
                wait_filled(act, label)
                A(dst, src, func, **kw).then_inc(done, 1)

            def take(label, dst, src, done, n, func=ACT.Copy, **kw):
                evac(label, dst, src, done, func, **kw)
                act.wait_ge(done, n)
                empty(act, label)

            take("gg", ggT, bk("gg")[0:RANK, 0:S], s["ggT_set"], 1)
            take("gq0", gq[:, 0:S], bk("gq0")[:, 0:S], s["gqk_set"], 1)
            take("gq1", gq[:, S:2 * S], bk("gq1")[:, 0:S], s["gqk_set"], 2)
            take("gk0", gk[:, 0:S], bk("gk0")[:, 0:S], s["gqk_set"], 3)
            take("gk1", gk[:, S:2 * S], bk("gk1")[:, 0:S], s["gqk_set"], 4)
            wait_filled(act, "z")
            for mt in range(2):
                last = A(zz[:, mt * S:(mt + 1) * S], bk("z")[:, mt * S:(mt + 1) * S], ACT.Identity,
                         bias=vcol("b_gla_gate", mt))
                last.then_inc(s["z_set"], 1)
            act.wait_ge(s["z_set"], 2)
            empty(act, "z")
            link(A(tt, zz, ACT.Abs))
            link(A(tt, tt, ACT.Exp, scale=-1.0))
            A(tt, tt, ACT.Ln, bias=1.0).then_inc(s["zl_set"], 1)
            take("gv0", gv[:, 0, :], bk("gv0"), s["gv_set"], 1)
            take("gv1", gv[:, 1, :], bk("gv1"), s["gv_set"], 2)
            for h in range(GH):
                wait_filled(act, f"gr{h}")
                A(gr[:, h, :], bk(f"gr{h}")[:, 0:S], ACT.Copy).then_inc(s["gr_set"], 1)
                act.wait_ge(s["gr_set"], h + 1)
                empty(act, f"gr{h}")
            A(flat(sgr), flat(gr), ACT.Sigmoid).then_inc(s["sgr_set"], 1)
            act.wait_ge(s["b_set"], 3)
            T16 = 1.0 / 16
            A(qe, zz, ACT.Exp, scale=T16).then_inc(s["e_set"], 1)
            A(ke, zz, ACT.Exp, scale=-T16).then_inc(s["e_set"], 1)
            A(kl, tt, ACT.Exp, scale=T16).then_inc(s["e_set"], 1)
            A(qb, bb, ACT.Exp, scale=T16).then_inc(s["e_set"], 1)
            A(dec, bb.rearrange("p (n t) -> p n t", t=CH)[:, :, CH - 1], ACT.Exp, scale=T16).then_inc(s["e_set"], 1)
            for m in range(4):
                take(f"mq{m}", mq[:, m, :], bk(f"mq{m}")[:, 0:S], s["mqk_set"], m + 1)
            for m in range(4):
                take(f"mk{m}", mk[:, m, :], bk(f"mk{m}")[:, 0:S], s["mqk_set"], 5 + m)
            take("klT", klnat, bk("klT"), s["klnat_set"], 1)
            act.wait_ge(s["attz_set"], 1)
            for par in range(2):
                wait_filled(act, f"att{par}")
                for np_ in (0, CH):
                    A(att[np_:np_ + CH, par::2, :, np_:np_ + CH],
                      bk(f"att{par}")[np_:np_ + CH, 0:2 * 2 * CH].rearrange("p (h pair q) -> p h pair q", h=2, pair=2),
                      ACT.Copy).then_inc(s["attd_set"], 1)
                act.wait_ge(s["attd_set"], 2 * par + 2)
                empty(act, f"att{par}")
            take("mv0", mv[:, 0, :], bk("mv0"), s["mv_set"], 1)
            take("mv1", mv[:, 1, :], bk("mv1"), s["mv_set"], 2)
            for i in range(2):
                wait_filled(act, f"o{i}")
                A(flat(oT[:, 2 * i:2 * i + 2, :]), bk(f"o{i}"), ACT.Copy).then_inc(s["o_set"], 1)
                A(osq[:, i * 512:(i + 1) * 512], bk(f"o{i}"), ACT.Square).then_inc(s["osq_set"], 1)
                act.wait_ge(s["o_set"], i + 1)
                act.wait_ge(s["osq_set"], i + 1)
                empty(act, f"o{i}")
            for i in range(2):
                take(f"gs{i}", rso[:, i * 512:(i + 1) * 512], bk(f"gs{i}"), s["gla_n"], i + 1, ACT.Sqrt,
                     bias=eps, scale=1.0 / GDV)
            for i in range(MH + 1):
                if i < MH:
                    act.wait_ge(s["max_set"], i + 1)
                    b = i % 2
                    for st in range(ST):
                        sl = scb[:, b, 0:P] if st == 0 else scb[:, b, P:P + S]
                        A(sl, sl, ACT.Exp, bias=mneg[:, 2 * b + st:2 * b + st + 1],
                          accum_out=rsum[:, 2 * b + st:2 * b + st + 1]).then_inc(s["exp_set"], 1)
                if i >= 1:
                    j = i - 1
                    if j >= 2:
                        act.wait_ge(filled[PLAN[f"pv{(j - 2) // 2}"][0]], PLAN[f"pv{(j - 2) // 2}"][1] + 1)
                    take(f"pT{j}", pTb[:, j % 2, :], bk(f"pT{j}")[:, 0:384], s["pT_set"], j + 1)

            act.wait_ge(s["eps_set"], 1)
            A(spare, eps, ACT.Sqrt)
            squares(s["xmid_set"], sq1, 0, s["sq1_set"])
            root("n_mlp", rstd1, s["n1_set"])
            for c in range(C):
                act.wait_ge(s["t1_set"], c + 1)
                A(hT[:, c, :], hT[:, c, :], ACT.Identity, bias=ada[:, 24 + c:25 + c]).then_inc(s["h_set"], 1)
            for m in range(FF // P):
                wait_filled(act, f"f{m}")
                A(h1[:, m, :], bk(f"f{m}")[:, 0:S], ACT.Relu).then_inc(s["relu_set"], 1)
                act.wait_ge(s["relu_set"], m + 1)
                inc_emptied(A(h1[:, m, :], h1[:, m, :], ACT.Square), f"f{m}")
            for c in range(C):
                act.wait_ge(s["x1_set"], c + 1)
                A(sq2[:, c, :], xT[:, c, :], ACT.Square).then_inc(s["sq2_set"], 1)
                A(sqg[:, c, :], xT[:, c, :], ACT.Square, scale=vcol("g_final", c)).then_inc(s["sq2_set"], 1)
            act.wait_ge(s["rr_set"], 1)
            A(rstd2, rstd2, ACT.Sqrt).then_inc(s["n3_set"], 1)
            A(lnr, bk("n_fin")[:, 0:S], ACT.Sqrt, bias=eps, scale=1.0 / D).then_inc(s["n2_set"], 1)
            act.wait_ge(s["n2_set"], 1)
            empty(act, "n_fin")
            for m in range(CT):
                wait_filled(act, f"cb{m}")
                if m >= 2:
                    act.wait_ge(s["up_set"], m - 1)
                take(f"cb{m}", sgb[:, m % 2, :], bk(f"cb{m}")[:, 0:S], s["sgb_set"], m + 1, ACT.Sigmoid)
            for m in range(8):
                if m >= 2:
                    act.wait_ge(s["pe_link"], m - 1)
                wait_filled(act, f"qk{m}")
                A(qsq[:, m % 2, :], bk(f"qk{m}")[:, 0:S], ACT.Square).then_inc(s["qsq_set"], 1)
                A(qk[:, m, :], bk(f"qk{m}")[:, 0:S], ACT.Copy).then_inc(s["qk_set"], 1)
                act.wait_ge(s["qk_set"], m + 1)
                act.wait_ge(s["qsq_set"], m + 1)
                empty(act, f"qk{m}")
                if m == 0:
                    act.wait_ge(s["up_set"], CT)
                for k in range(4 * m, min(4 * m + 4, TAPS)):
                    if k > 4:
                        act.wait_ge(s["conv_pool_set"], k - 4)
                    tap = cw[:, (CT - 1) * TAPS + k:(CT - 1) * TAPS + k + 1]
                    if k == 0:
                        ins = A(mix2[:, C - 1, :], up[:, CT - 1, k:k + S], ACT.Identity, scale=tap,
                                bias=vcol("conv_dw_b_2", CT - 1))
                    else:
                        ins = A(tapped[:, k % 4, :], up[:, CT - 1, k:k + S], ACT.Copy, scale=tap)
                    ins.then_inc(s["tap_set"], 1)
            wait_filled(act, "qs")
            A(rs16, bk("qs")[0:16, 0:S], ACT.Sqrt, bias=eps[0:16, :], scale=1.0 / HD).then_inc(s["rs16_set"], 1)
            act.wait_ge(s["rs16_set"], 1)
            empty(act, "qs")
            take("v0", vn[:, 0, :], bk("v0"), s["v_set"], 1)
            act.wait_ge(s["cmean_set"], 1)
            A(flat(csq), flat(mix2[:, 4:8, :]), ACT.Square).then_inc(s["csq_set"], 1)
            take("v1", vn[:, 1, :], bk("v1"), s["v_set"], 2)
            wait_filled(act, "cv")
            A(lnr, bk("cv")[:, 0:S], ACT.Sqrt, bias=eps, scale=1.0 / CW).then_inc(s["cvar_set"], 1)
            act.wait_ge(s["cvar_set"], 1)
            empty(act, "cv")
            for i in range(MH + 2):
                if i < MH:
                    act.wait_ge(s["tmax_set"], i + 1)
                    for st in range(ST):
                        sl = tcb[i % 3][:, st * S:(st + 1) * S]
                        A(sl, sl, ACT.Exp, bias=mneg[:, 2 * (i % 2) + st:2 * (i % 2) + st + 1])\
                            .then_inc(s["texp_set"], 1)
                if i >= 2:
                    j = i - 2
                    if j >= 2:
                        act.wait_ge(filled[PLAN[f"pw{(j - 2) // 2}"][0]], PLAN[f"pw{(j - 2) // 2}"][1] + 1)
                    take(f"uT{j}", uTb[:, j % 2, :], bk(f"uT{j}"), s["uT_set"], j + 1)
                if 1 <= i <= MH:
                    j = i - 1
                    act.wait_ge(s["tm_set"], j + 1)
                    for st in range(ST):
                        sl = tcb[j % 3][:, st * S:(st + 1) * S]
                        A(sl, sl, ACT.Copy, scale=rinv[:, 2 * (j % 2) + st:2 * (j % 2) + st + 1])\
                            .then_inc(s["tp_set"], 1)
                if i == 5:
                    act.wait_ge(s["cln_set"], CT)
                    A(flat(csq), flat(mix2[:, 4:8, :]), ACT.Sigmoid).then_inc(s["csg_set"], 1)
            A(spare, eps, ACT.Sqrt)
            squares(s["x2_set"], sq2, 0, s["sq3_set"])
            root("n_two", rstd2, s["n4_set"])
            A(spare, eps, ACT.Exp)
            act.wait_ge(s["lg_set"], 1)
            A(flat(aff), flat(aff), ACT.Exp).then_inc(s["lge_set"], 1)
            for i in range(4):
                wait_filled(act, f"hn{i}")
                for st in range(ST):
                    src = bk(f"hn{i}").rearrange("p (c st d) -> p c st d", c=2, st=ST)[:, :, st, :]
                    A(hnat[:, st, 2 * i * P:(2 * i + 2) * P].rearrange("p (c d) -> p c d", c=2), src,
                      ACT.Copy).then_inc(s["hnat_set"], 1)
                act.wait_ge(s["hnat_set"], 2 * i + 2)
                empty(act, f"hn{i}")
            for i in range(4):
                wait_filled(act, f"xf{i}")
                for st in range(ST):
                    src = bk(f"xf{i}").rearrange("p (c st d) -> p c st d", c=2, st=ST)[:, :, st, :]
                    A(yacc[:, st, 2 * i * P:(2 * i + 2) * P].rearrange("p (c d) -> p c d", c=2), src,
                      ACT.Copy).then_inc(s["yinit_set"], 1)
                act.wait_ge(s["yinit_set"], 2 * i + 2)
                empty(act, f"xf{i}")

            act.sem_inc(s["xe_set"], 1)
            act.sem_inc(s["ye_set"], 1)
            with act.Fori(0, NE) as e:
                act.wait_ge(s["xe_full"], e + 1)
                A(flat(xe), ps[:, 7, 0:S], ACT.Copy).then_inc(s["xe_set"], 1)
                act.wait_ge(s["pgT_full"], e + 2)
                act.wait_ge(s["sc_full"], 1 + 4 * e)
                A(pgT, ps[:, 4, 0:S], ACT.Copy).then_inc(s["pgT_set"], 1)
                act.wait_ge(s["h1_full"], e + 1)
                act.wait_ge(s["he_set"], 1 + 2 * e)
                A(sge.rearrange("p (a b) -> p a b", a=2), ps[:, 0:2, 0:FH], ACT.Sigmoid).then_inc(s["sg_set"], 1)
                act.wait_ge(s["ye_full"], e + 1)
                A(ye, ps[:, 4, 0:DG], ACT.Copy).then_inc(s["ye_set"], 1)
            o_rows = out.rearrange("b (st p) d -> p (b st) d", p=P)
            for j in range(4):
                act.wait_ge(s["sc_used"], 1 + 4 * (NE - 1) + j + 1)
                act.dma_start(o_rows[:, :, j * DG:(j + 1) * DG], yacc[:, :, j * DG:(j + 1) * DG])\
                    .then_inc(s["out_done"], 16)
            act.wait_ge(s["out_done"], 16 * 4)

        @block.vector
        def _(dve):
            V = nc.vector
            n_link = [0]

            def link(ins):
                n_link[0] += 1
                ins.then_inc(s["dve_link"], 1)
                dve.wait_ge(s["dve_link"], n_link[0])

            dve.wait_ge(s["cact_set"], 1)
            V.tensor_tensor(cact, sg8, cols[:, VEC["c"][0]:VEC["c"][0] + C], ALU.mult).then_inc(s["adacol_set"], 1)
            V.memset(rtb[:, S:384], NEG).then_inc(s["rtbneg_set"], 1)
            dve.wait_ge(s["n0_set"], 1)
            link(V.reciprocal(rstd0, rstd0))

            def ada_rows(k):
                wait_filled(dve, f"ada{k}")
                V.tensor_copy(adarow, bk(f"ada{k}")[:, 0:S]).then_inc(s["adarow_set"], 1)
                dve.wait_ge(s["adarow_set"], k + 1)
                empty(dve, f"ada{k}")

            def ada_cols(k):
                wait_filled(dve, f"at{k}")
                b0 = VEC["b_ada"][0] + C * k
                link(V.tensor_tensor(ada[:, C * k:C * k + C].rearrange("p (j h) -> p h j", h=2),
                                     bk(f"at{k}")[:, 0:S].rearrange("p (h j q) -> p h j q", h=2, j=4)[:, :, :, 0],
                                     cols[:, b0:b0 + C].rearrange("p (j h) -> p h j", h=2), ALU.add))
                empty(dve, f"at{k}")

            for k in range(2):
                ada_rows(k)
                ada_cols(k)
            g0 = VEC["g_mix"][0]
            V.scalar_tensor_tensor(amix, ada[:, C:2 * C], 1.0, cols[:, g0:g0 + C], ALU.add, ALU.mult)\
                .then_inc(s["amix_set"], 1)
            dve.wait_ge(s["amix_set"], 1)
            for c in range(C):
                V.scalar_tensor_tensor(hT[:, c, :], xT[:, c, :], amix[:, c:c + 1], rstd0, ALU.mult, ALU.mult)\
                    .then_inc(s["t0_set"], 1)

            for i in range(4):
                wait_filled(dve, f"wf{i}")
                inc_emptied(V.tensor_copy(flat(relW[:, 2 * i:2 * i + 2, :]), bk(f"wf{i}")), f"wf{i}")
            dve.wait_ge(s["zl_set"], 1)
            link(V.scalar_tensor_tensor(zz, zz, 0.0, tt, ALU.min, ALU.subtract))
            dve.wait_ge(s["scan_set"], 1)
            link(V.tensor_tensor_scan(bb, scanm, zz, 0.0, ALU.mult, ALU.add))
            b3, z3, t3 = (a.rearrange("p (n t) -> p n t", t=CH) for a in (bb, zz, tt))
            V.tensor_tensor(z3, b3, b3[:, :, CH // 2 - 1:CH // 2].broadcast_to([P, 2 * NCH, CH]), ALU.subtract)\
                .then_inc(s["b_set"], 1)
            V.tensor_tensor(t3, b3[:, :, CH - 1:CH].broadcast_to([P, 2 * NCH, CH]), b3, ALU.subtract)\
                .then_inc(s["b_set"], 1)
            dve.wait_ge(s["b_set"], 2)
            dve.sem_inc(s["b_set"], 1)
            dve.wait_ge(s["e_set"], 4)
            dve.wait_ge(s["gqk_set"], 4)
            V.scalar_tensor_tensor(qe, qe, GDK ** -0.5, gq, ALU.mult, ALU.mult).then_inc(s["gla_set"], 1)
            V.tensor_tensor(ke, ke, gk, ALU.mult).then_inc(s["gla_set"], 1)
            V.tensor_tensor(kl, kl, gk, ALU.mult).then_inc(s["gla_set"], 1)
            dve.wait_ge(s["qb1z_set"], 1)
            V.scalar_tensor_tensor(qb1[CH:P, :], qb[CH:P, :], GDK ** -0.5, gq[CH:P, :], ALU.mult, ALU.mult)\
                .then_inc(s["gla_set"], 1)
            V.scalar_tensor_tensor(qb[0:CH, :], qb[0:CH, :], GDK ** -0.5, gq[0:CH, :], ALU.mult, ALU.mult)\
                .then_inc(s["gla_set"], 1)
            dve.wait_ge(s["gla_set"], 5)
            V.memset(qb[CH:P, :], 0.0).then_inc(s["gla_set"], 1)
            dve.wait_ge(s["sgr_set"], 1)
            link(V.tensor_tensor(flat(gr), flat(gr), flat(sgr), ALU.mult))
            wait_filled(dve, "kv0")
            kv0 = bk("kv0").rearrange("p (n m v) -> p n m v", n=2, m=2)
            kv1 = bk("kv1")[:, 0:S].rearrange("p (m v) -> p m v", m=2)
            link(V.tensor_copy(Sst[:, 0, :, :], kv0[:, 0, :, :]))
            dve.wait_ge(s["e_set"], 5)
            wait_filled(dve, "kv1")
            for mt in range(2):
                link(V.scalar_tensor_tensor(S_at(Sst, 1, mt), S_at(Sst, 0, mt), dec[:, NCH * mt + 1:NCH * mt + 2],
                                            kv1[:, mt, :], ALU.mult, ALU.add))
            empty(dve, "kv1")
            for mt in range(2):
                link(V.scalar_tensor_tensor(S_at(Sst, 2, mt), S_at(Sst, 1, mt), dec[:, NCH * mt + 2:NCH * mt + 3],
                                            kv0[:, 1, mt, :], ALU.mult, ALU.add))
            empty(dve, "kv0")
            dve.sem_inc(s["S_set"], 1)
            def gla_root(i):
                dve.wait_ge(s["gla_n"], i + 1)
                link(V.reciprocal(rso[:, i * 512:(i + 1) * 512], rso[:, i * 512:(i + 1) * 512]))

            def gla_finish():
                for h in range(GH):
                    ins = V.scalar_tensor_tensor(oT[:, h, :], oT[:, h, :], vcol("g_gla_out", h),
                                                 rso[:, h * S:(h + 1) * S], ALU.mult, ALU.mult)
                link(ins)
                for h in range(GH):
                    V.tensor_tensor(mix[:, h, :], oT[:, h, :], gr[:, h, :], ALU.mult).then_inc(s["mixg_set"], 1)

            dve.wait_ge(emptied[PLAN["wf3"][0]], PLAN["wf3"][1] + 1)
            for i in range(MH + 2):
                if i < MH:
                    b = i % 2
                    wait_filled(dve, f"sc{i}")
                    if i >= 2:
                        wait_filled(dve, f"pT{i - 2}")
                    V.scalar_tensor_tensor(scb[:, b, 0:P], bk(f"sc{i}")[:, 0:P], HD ** -0.5, relW[:, i, P:2 * P],
                                           ALU.mult, ALU.add)
                    link(V.scalar_tensor_tensor(scb[:, b, P:P + S], bk(f"sc{i}")[:, P:P + S], HD ** -0.5,
                                                relW[:, i, :], ALU.mult, ALU.add))
                    V.reduce_max(mx[:, 0:1], scb[:, b, 0:P], AX.X)
                    link(V.reduce_max(mx[:, 1:2], scb[:, b, P:P + S], AX.X))
                    empty(dve, f"sc{i}")
                    V.tensor_scalar(mneg[:, 2 * b:2 * b + 2], mx, -1.0, None, ALU.mult).then_inc(s["max_set"], 1)
                    if i in (2, 4):
                        gla_root(i // 2 - 1)
                    if i == 6:
                        gla_finish()
                    (ada_rows, ada_cols)[i % 2](2 + i // 2)
                if 1 <= i <= MH:
                    b = (i - 1) % 2
                    dve.wait_ge(s["exp_set"], 2 * i)
                    link(V.reciprocal(rinv[:, 2 * b:2 * b + 2], rsum[:, 2 * b:2 * b + 2]))
                    V.tensor_scalar(scb[:, b, 0:P], scb[:, b, 0:P], rinv[:, 2 * b:2 * b + 1], None, ALU.mult)
                    V.tensor_scalar(scb[:, b, P:P + S], scb[:, b, P:P + S], rinv[:, 2 * b + 1:2 * b + 2], None,
                                    ALU.mult).then_inc(s["p_set"], 1)
                if i >= 3 and i % 2 == 1:
                    p = (i - 3) // 2
                    wait_filled(dve, f"pv{p}")
                    inc_emptied(V.tensor_copy(mix[:, 4 + p, :], bk(f"pv{p}")[:, 0:S]), f"pv{p}")
                    dve.wait_ge(emptied[PLAN[f"pv{p}"][0]], PLAN[f"pv{p}"][1] + 1)
                    dve.sem_inc(s["mixm_set"], 1)
            g1 = VEC["g_mlp"][0]
            link(V.scalar_tensor_tensor(amlp, ada[:, 4 * C:5 * C], 1.0, cols[:, g1:g1 + C], ALU.add, ALU.mult))

            def add_gated(label, gate, done):
                for m in range(C):
                    wait_filled(dve, f"{label}{m}")
                    V.scalar_tensor_tensor(xT[:, m, :], bk(f"{label}{m}")[:, 0:S], gate[:, m:m + 1], xT[:, m, :],
                                           ALU.mult, ALU.add).then_inc(done, 1)
                    dve.wait_ge(done, m + 1)
                    empty(dve, f"{label}{m}")

            def normed(dst, rstd, gains, root_done, done):
                dve.wait_ge(root_done, 1)
                link(V.reciprocal(rstd, rstd))
                for c in range(C):
                    V.scalar_tensor_tensor(dst[:, c, :], xT[:, c, :], gains[:, c:c + 1], rstd, ALU.mult, ALU.mult)\
                        .then_inc(done, 1)

            def gains(name):
                return cols[:, VEC[name][0]:VEC[name][0] + C]

            add_gated("y", ada[:, 2 * C:3 * C], s["xmid_set"])
            normed(hT, rstd1, amlp, s["n1_set"], s["t1_set"])
            add_gated("g", ada[:, 5 * C:6 * C], s["x1_set"])
            link(V.tensor_tensor(gg2, gains("g_final"), gains("norm1_g_2"), ALU.mult))
            wait_filled(dve, "n_fin")
            wait_filled(dve, "n_one")
            link(V.tensor_scalar(rstd2, bk("n_fin")[:, 0:S], EPS / D, EPS * EPS, ALU.mult, ALU.add))
            V.scalar_tensor_tensor(rstd2, bk("n_one")[:, 0:S], 1.0 / D, rstd2, ALU.mult, ALU.add)\
                .then_inc(s["rr_set"], 1)
            dve.wait_ge(s["rr_set"], 1)
            empty(dve, "n_one")
            normed(hT, rstd2, gg2, s["n3_set"], s["h2_set"])
            normed(xT, lnr, gains("g_final"), s["n2_set"], s["xf_set"])
            dve.wait_ge(s["xf_set"], C)

            dve.wait_ge(s["upz_set"], 1)
            for m in range(CT):
                wait_filled(dve, f"ca{m}")
                dve.wait_ge(s["sgb_set"], m + 1)
                V.tensor_tensor(up[:, m, PAD:PAD + S], bk(f"ca{m}")[:, 0:S], sgb[:, m % 2, :], ALU.mult)\
                    .then_inc(s["up_set"], 1)
                dve.wait_ge(s["up_set"], m + 1)
                empty(dve, f"ca{m}")
            n_conv = 0
            for k in range(TAPS):
                for m in range(CT - 1):
                    src = up[:, m, k:k + S]
                    tap = cw[:, m * TAPS + k:m * TAPS + k + 1]
                    dst = mix2[:, 4 + m, :]
                    if k == 0:
                        ins = V.tensor_scalar(dst, src, tap, vcol("conv_dw_b_2", m), ALU.mult, ALU.add)
                    else:
                        dve.wait_ge(s["conv_set"], n_conv - (CT - 1) + 1)
                        ins = V.scalar_tensor_tensor(dst, src, tap, dst, ALU.mult, ALU.add)
                    ins.then_inc(s["conv_set"], 1)
                    n_conv += 1
            dve.wait_ge(s["rs16_set"], 1)
            V.reciprocal(rs16, rs16).then_inc(s["rs16i_set"], 1)
            dve.wait_ge(s["consts2_in"], 32)
            dve.wait_ge(s["qk_set"], 8)

            def pair_of(p):
                return flat(qk[:, 2 * p:2 * p + 2, :])

            def gained(p):
                wait_filled(dve, f"bc{p}")
                V.scalar_tensor_tensor(pair_of(p), pair_of(p), vcol("q_norm_g_2" if p < 2 else "k_norm_g_2", 0),
                                       bk(f"bc{p}"), ALU.mult, ALU.mult).then_inc(s["qn_set"], 1)
                dve.wait_ge(s["qn_set"], p + 1)
                empty(dve, f"bc{p}")

            def rotated(p):
                wait_filled(dve, f"rt{p}")
                V.tensor_tensor(qt[:, p % 2, :], bk(f"rt{p}"), sin2, ALU.mult).then_inc(s["rt_set"], 1)
                link(V.tensor_tensor(pair_of(p), pair_of(p), cos2, ALU.mult))
                dve.wait_ge(s["rt_set"], p + 1)
                empty(dve, f"rt{p}")
                V.tensor_tensor(pair_of(p), pair_of(p), qt[:, p % 2, :], ALU.add).then_inc(s["qf_set"], 1)

            dve.wait_ge(s["conv_pool_set"], TAPS - 1)
            gained(0)
            gained(1)
            wait_filled(dve, "cm")
            V.tensor_scalar(lnr, bk("cm")[:, 0:S], 1.0 / CW, None, ALU.mult).then_inc(s["cm_set"], 1)
            dve.wait_ge(s["cm_set"], 1)
            empty(dve, "cm")
            for p in range(4):
                rotated(p)
                if p < 2:
                    gained(p + 2)

            dve.wait_ge(s["neg_set"], 1)
            for i in range(MH + 3):
                if i < MH:
                    b, buf = i % 2, tcb[i % 3]
                    wait_filled(dve, f"tc{i}")
                    if i >= 3:
                        wait_filled(dve, f"uT{i - 3}")
                    link(V.scalar_tensor_tensor(buf, bk(f"tc{i}"), HD ** -0.5, neg2, ALU.mult, ALU.add))
                    empty(dve, f"tc{i}")
                    link(V.reduce_max(mx, buf.rearrange("p (st k) -> p st k", st=ST), AX.X))
                    V.tensor_scalar(mneg[:, 2 * b:2 * b + 2], mx, -1.0, None, ALU.mult).then_inc(s["tmax_set"], 1)
                if 1 <= i <= MH:
                    b, buf = (i - 1) % 2, tcb[(i - 1) % 3]
                    dve.wait_ge(s["texp_set"], 2 * i)
                    for st in range(ST):
                        sl = buf[:, st * S:(st + 1) * S]
                        ins = V.scalar_tensor_tensor(sl, sl, 1.0, cnt2[:, st * S:(st + 1) * S], ALU.mult, ALU.mult,
                                                     accum_out=rsum[:, 2 * b + st:2 * b + st + 1])
                    link(ins)
                    V.reciprocal(rinv[:, 2 * b:2 * b + 2], rsum[:, 2 * b:2 * b + 2]).then_inc(s["tm_set"], 1)
                if i >= 4 and i % 2 == 0:
                    p = (i - 4) // 2
                    wait_filled(dve, f"pw{p}")
                    inc_emptied(V.tensor_copy(mix2[:, p, :], bk(f"pw{p}")[:, 0:S]), f"pw{p}")
                    dve.wait_ge(emptied[PLAN[f"pw{p}"][0]], PLAN[f"pw{p}"][1] + 1)
                    dve.sem_inc(s["mixa_set"], 1)
                if i == 1:
                    dve.wait_ge(s["cvar_set"], 1)
                    V.reciprocal(lnr, lnr).then_inc(s["crec_set"], 1)
            for m in range(C):
                wait_filled(dve, f"z{m}")
                V.tensor_tensor(xT[:, m, :], bk(f"z{m}")[:, 0:S], xT[:, m, :], ALU.add).then_inc(s["x2_set"], 1)
                dve.wait_ge(s["x2_set"], m + 1)
                empty(dve, f"z{m}")
            normed(hT, rstd2, gains("norm2_g_2"), s["n4_set"], s["h3_set"])

            wait_filled(dve, "lg")
            link(V.reduce_max(rmx, bk("lg")[:, 0:2 * NE].rearrange("p (st e) -> p st e", st=ST), AX.X))
            for st in range(ST):
                ins = V.tensor_scalar(aff[:, st, :], bk("lg")[:, st * NE:(st + 1) * NE], rmx[:, st:st + 1], None,
                                      ALU.subtract)
            link(ins)
            empty(dve, "lg")
            dve.sem_inc(s["lg_set"], 1)
            dve.wait_ge(s["lge_set"], 1)
            link(V.reduce_sum(rsm, aff, AX.X))
            link(V.reciprocal(rsm, rsm))
            for st in range(ST):
                ins = V.tensor_scalar(aff[:, st, :], aff[:, st, :], rsm[:, st:st + 1], None, ALU.mult)
            ins.then_inc(s["aff_set"], 1)
            dve.wait_ge(s["aff_set"], 1)
            dve.wait_ge(s["consts3_in"], 16)
            wait_filled(dve, "aT")
            link(V.tensor_copy(affT, bk("aT")[0:NE, 0:S]))
            empty(dve, "aT")
            for k in range(CAP // 8):
                rest = affT if k == 0 else restT
                link(V.max(top8, rest))
                if k < CAP // 8 - 1:
                    link(V.match_replace(restT, top8, rest, -1.0))
            V.tensor_scalar(equalT, affT, top8[:, 7:8], None, ALU.is_equal)
            link(V.tensor_scalar(aboveT, affT, top8[:, 7:8], None, ALU.is_gt, ALU.add, accum_out=n_above))
            V.tensor_scalar(room, n_above, -1.0, float(CAP), ALU.mult, ALU.add)
            link(V.tensor_tensor_scan(countT, equalT, equalT, 0.0, ALU.add, ALU.max))
            link(V.scalar_tensor_tensor(equalT, countT, room, equalT, ALU.is_le, ALU.mult))
            link(V.tensor_tensor_scan(countT, aboveT, equalT, 0.0, ALU.add, ALU.add))
            link(V.tensor_tensor(aboveT, aboveT, equalT, ALU.add))
            V.tensor_tensor(placeT, aboveT, countT, ALU.mult).then_inc(s["place_set"], 1)
            wait_filled(dve, "rk")
            link(V.tensor_copy(flat(place), bk("rk")[:, 0:ST * NE]))
            empty(dve, "rk")
            for st in range(ST):
                ins = V.tensor_tensor(pick[:, st, :].rearrange("p (e t) -> p e t", e=NE),
                                      iota.unsqueeze(1).broadcast_to([P, NE, CAP]),
                                      place[:, st, :].unsqueeze(2).broadcast_to([P, NE, CAP]), ALU.is_equal)
            ins.then_inc(s["rank_set"], 1)
            dve.wait_ge(s["rank_set"], 1)
            dve.sem_inc(s["pick_set"], 1)
            dve.wait_ge(s["yinit_set"], 8)

            dve.sem_inc(s["he_set"], 1)
            dve.sem_inc(s["sc_used"], 1)
            with dve.Fori(0, NE) as e:
                dve.wait_ge(s["sg_set"], e + 1)
                V.tensor_tensor(he.rearrange("p (a b) -> p a b", a=2), sge.rearrange("p (a b) -> p a b", a=2),
                                ps[:, 0:2, 0:FH], ALU.mult).then_inc(s["he_set"], 1)
                dve.wait_ge(s["h3_full"], e + 1)
                dve.wait_ge(s["he_set"], 2 * e + 2)
                V.tensor_tensor(he.rearrange("p (a b) -> p a b", a=2), he.rearrange("p (a b) -> p a b", a=2),
                                ps[:, 2:4, 0:FH], ALU.mult).then_inc(s["he_set"], 1)
                dve.wait_ge(s["he_set"], 2 * e + 3)
                V.transpose(hTe, he.rearrange("p (q r) -> p r q", r=FR)).then_inc(s["hTe_set"], 1)
                for j in range(4):
                    dve.wait_ge(s["sc_full"], 4 * e + j + 2)
                    V.tensor_tensor(yacc[:, :, j * DG:(j + 1) * DG], yacc[:, :, j * DG:(j + 1) * DG],
                                    ps[:, 5 + j % 2, :].rearrange("p (st n) -> p st n", st=ST), ALU.add)\
                        .then_inc(s["sc_used"], 1)

        @block.tensor
        def _(pe):
            def mm(o, w, x, first, last):
                return pe.matmul(o, w, x, start=first, stop=last)

            pe.wait_ge(s["small_in"], 16 * 8)
            inc_filled(mm(bk("rel")[0:MH, 0:384], relst, onehot, True, True), "rel")

            def turn(label, src_of):
                wait_emptied(pe, label)
                for k in range(2):
                    for st in range(ST):
                        ins = pe.transpose(bk(label)[:, (2 * k + st) * P:(2 * k + st + 1) * P], src_of(k, st),
                                           ident[:, :])
                inc_filled(ins, label)

            def norm_sum(label, sq, done):
                wait_emptied(pe, label)
                for c in range(C):
                    pe.wait_ge(done, c + 1)
                    ins = mm(bk(label)[:, 0:S], ones[:, :], sq[:, c, :], c == 0, c == C - 1)
                inc_filled(ins, label)

            pe.wait_ge(s["ones_set"], 1)
            norm_sum("n_in", sq0, s["sq0_set"])

            def ada_part(k):
                wait_unit(pe, f"ada{k}")
                wait_emptied(pe, f"ada{k}")
                w = unit_ap(f"ada{k}", C, D)
                for c in range(C):
                    for j in range(4):
                        ins = mm(bk(f"ada{k}")[32 * j:32 * j + 32, 0:DG], cact[:, c:c + 1].broadcast_to([P, 32]),
                                 w[:, c, j * DG:(j + 1) * DG], c == 0, c == C - 1)
                finish(f"ada{k}", ins)

            def ada_turn(k):
                wait_emptied(pe, f"at{k}")
                pe.wait_ge(s["adarow_set"], k + 1)
                for half in range(2):
                    ins = pe.transpose(bk(f"at{k}")[:, half * P:(half + 1) * P], adarow[:, half * P:(half + 1) * P],
                                       ident[:, :])
                inc_filled(ins, f"at{k}")

            def used(ins):
                ins.then_inc(s["unit_used"], 1)

            def bank_done(label):
                pe.sem_inc(filled[PLAN[label][0]], 1)

            pe.wait_ge(s["adacol_set"], 1)
            n_used = [0]

            def finish(label, ins):
                used(ins)
                n_used[0] += 1
                pe.wait_ge(s["unit_used"], n_used[0])
                bank_done(label)

            for k in range(2):
                ada_part(k)
                ada_turn(k)

            def proj(label, w, m0, x, wait=None, n=P, k=C, last=False, after=None):
                wait_emptied(pe, label)
                for c in range(k):
                    if wait is not None:
                        pe.wait_ge(wait, c + 1)
                    ins = mm(bk(label)[0:n, 0:S], w[:, c, m0:m0 + n], x[:, c, :], c == 0, c == k - 1)
                if last:
                    finish(label, ins)
                else:
                    inc_filled(ins, label)

            def proj_rows(label, w, c0, x, st, last=False):
                wait_emptied(pe, label)
                for c in range(C):
                    ins = mm(bk(label), x[:, c, st * P:(st + 1) * P], w[:, c, c0:c0 + 512], c == 0, c == C - 1)
                if last:
                    finish(label, ins)
                else:
                    inc_filled(ins, label)

            wait_unit(pe, "win_a")
            pe.wait_ge(unit_in2, 16)
            w = unit_ap("win_a", C, 512)
            o = (UNIT["win_a"] % 3) * BLOCK + C * 512
            wg = ring[:, o:o + C * RANK].rearrange("p (c n) -> p c n", c=C)
            proj("gg", wg, 0, hT, s["hT_set"], n=RANK)
            proj("gq0", w, 0, hT)
            proj("gq1", w, P, hT)
            proj("gk0", w, 2 * P, hT)
            proj("gk1", w, 3 * P, hT, last=True)
            pe.wait_ge(s["ggT_set"], 1)
            wait_emptied(pe, "z")
            for mt in range(2):
                ins = mm(bk("z")[:, mt * S:(mt + 1) * S], wgate[:, mt * P:(mt + 1) * P], ggT, True, True)
            inc_filled(ins, "z")
            pe.wait_ge(s["relW_in"], 16)
            for i in range(4):
                wait_emptied(pe, f"wf{i}")
                inc_filled(mm(bk(f"wf{i}"), flip, flat(relR[:, 2 * i:2 * i + 2, :]), True, True), f"wf{i}")
            wait_unit(pe, "win_b")
            w = unit_ap("win_b", C, 1024)
            for st in range(ST):
                proj_rows(f"gv{st}", w, 0, hT, st)
            for h in range(GH):
                proj(f"gr{h}", w, 512 + h * P, hT, last=(h == GH - 1))
            wait_unit(pe, "win_c")
            w = unit_ap("win_c", C, 1024)
            for m in range(4):
                proj(f"mq{m}", w, m * P, hT)
            for m in range(4):
                proj(f"mk{m}", w, 512 + m * P, hT, last=(m == 3))
            pe.wait_ge(s["gla_set"], 6)
            turn("klT", lambda k, st: kl[:, k * S + st * P:k * S + (st + 1) * P])
            for par in range(2):
                hp = GDK * par
                wait_emptied(pe, f"att{par}")
                for k in range(2):
                    for n in range(NCH):
                        np_ = CH * (n % 2)
                        t0 = k * S + n * CH
                        o0 = (k * 2 + n // 2) * CH
                        ins = mm(bk(f"att{par}")[np_:np_ + CH, o0:o0 + CH], ke[hp:hp + GDK, t0:t0 + CH],
                                 qe[hp:hp + GDK, t0:t0 + CH], True, True)
                inc_filled(ins, f"att{par}")
            pe.wait_ge(s["klnat_set"], 1)
            pe.wait_ge(s["gv_set"], 2)
            for label, chunks in (("kv0", (0, 2)), ("kv1", (1,))):
                wait_emptied(pe, label)
                for n in chunks:
                    for h in range(GH):
                        hp, np_ = GDK * (h % 2), CH * (n % 2)
                        k0 = ((h // 2) * 2 + n // 2) * P + hp
                        o0 = ((n // 2) * 2 + h // 2) * GDV
                        ins = mm(bk(label)[hp:hp + GDK, o0:o0 + GDV], klnat[np_:np_ + CH, k0:k0 + GDK],
                                 gv[np_:np_ + CH, n // 2, h * GDV:(h + 1) * GDV], True, True)
                inc_filled(ins, label)
            wait_unit(pe, "win_d")
            w = unit_ap("win_d", C, 512)
            for st in range(ST):
                proj_rows(f"mv{st}", w, 0, hT, st, last=(st == 1))
            pe.wait_ge(s["att_set"], GH)
            pe.wait_ge(s["S_set"], 1)
            for h in range(GH):
                label = f"o{h // 2}"
                if h % 2 == 0:
                    wait_emptied(pe, label)
                o_ap = bk(label)[:, (h % 2) * S:(h % 2) * S + S]
                for pair in range(2):
                    mm(o_ap[:, pair * P:(pair + 1) * P], gv[:, pair, h * GDV:(h + 1) * GDV], att[:, h, pair, :],
                       True, False)
                    for n in range(max(1, 2 * pair), 2 * pair + 2):
                        t0 = (h // 2) * S + n * CH
                        ins = mm(o_ap[:, n * CH:(n + 1) * CH], S_at(Sst, n - 1, h // 2),
                                 (qb, qb1)[h % 2][:, t0:t0 + CH], False, n % 2 == 1)
                if h % 2:
                    inc_filled(ins, label)
            for i in range(2):
                pe.wait_ge(s["osq_set"], i + 1)
                wait_emptied(pe, f"gs{i}")
                inc_filled(mm(bk(f"gs{i}"), ones[:, :], osq[:, i * 512:(i + 1) * 512], True, True), f"gs{i}")

            pe.wait_ge(s["mqk_set"], 8)
            for i in range(MH + 2):
                for j in (0, 1) if i == 0 else (i + 1,):
                    if j < MH:
                        hp, mt = 64 * (j % 2), j // 2
                        wait_emptied(pe, f"sc{j}")
                        mm(bk(f"sc{j}")[:, 0:P], mq[hp:hp + HD, mt, 0:P], mk[hp:hp + HD, mt, 0:P], True, True)
                        inc_filled(mm(bk(f"sc{j}")[:, P:P + S], mq[hp:hp + HD, mt, P:2 * P], mk[hp:hp + HD, mt, :],
                                      True, True), f"sc{j}")
                if i < MH:
                    (ada_part, ada_turn)[i % 2](2 + i // 2)
                if 1 <= i <= MH:
                    j = i - 1
                    b = j % 2
                    pe.wait_ge(s["p_set"], j + 1)
                    wait_emptied(pe, f"pT{j}")
                    pe.transpose(bk(f"pT{j}")[:, 0:P], scb[:, b, 0:P], ident[:, :])
                    pe.transpose(bk(f"pT{j}")[:, P:2 * P], scb[:, b, P:2 * P], ident[:, :])
                    inc_filled(pe.transpose(bk(f"pT{j}")[:, 2 * P:3 * P], scb[:, b, 2 * P:3 * P], ident[:, :]),
                               f"pT{j}")
                if i >= 2:
                    j = i - 2
                    hp = 64 * (j % 2)
                    label = f"pv{j // 2}"
                    if j % 2 == 0:
                        wait_emptied(pe, label)
                    pe.wait_ge(s["pT_set"], j + 1)
                    pe.wait_ge(s["mv_set"], 2)
                    pt = pTb[:, j % 2, :]
                    mm(bk(label)[hp:hp + HD, 0:S], mv[:, 0, j * HD:(j + 1) * HD], pt[:, 0:S], True, False)
                    ins = mm(bk(label)[hp:hp + HD, P:S], mv[:, 1, j * HD:(j + 1) * HD], pt[:, S:384], False, True)
                    if j % 2:
                        inc_filled(ins, label)

            def out_proj(y, n_label, w_of, x, ready, sq, sq_done, units):
                def square_sum(c):
                    if c == 0:
                        wait_emptied(pe, n_label)
                    pe.wait_ge(sq_done, c + 1)
                    ins = mm(bk(n_label)[:, 0:S], ones[:, :], sq[:, c, :], c == 0, c == C - 1)
                    if c == C - 1:
                        inc_filled(ins, n_label)

                for m in range(C):
                    w, m0, last = w_of(m)
                    if m == 0:
                        ready()
                    if m in units:
                        wait_unit(pe, units[m])
                    proj(f"{y}{m}", w, m0, x, last=last)
                    if m >= 2:
                        square_sum(m - 2)
                square_sum(C - 2)
                square_sum(C - 1)

            def mixed():
                pe.wait_ge(s["mixg_set"], GH)
                pe.wait_ge(s["mixm_set"], 4)

            w = unit_ap("wout", C, D)
            out_proj("y", "n_mlp", lambda m: (w, m * P, m == C - 1), mix, mixed, sq1, s["sq1_set"], {0: "wout"})
            for u in range(4):
                wait_unit(pe, f"ff1_{u}")
                w = unit_ap(f"ff1_{u}", C, D)
                for m in range(C):
                    proj(f"f{C * u + m}", w, m * P, hT, s["h_set"] if u == 0 and m == 0 else None, last=(m == C - 1))
            for u in range(4):
                wait_unit(pe, f"ff2_{u}")
                w = unit_ap(f"ff2_{u}", C, D)
                for m in range(C):
                    if u == 0:
                        wait_emptied(pe, f"g{m}")
                    if u == 0 and m == 0:
                        for b in range(8):
                            pe.wait_ge(emptied[b], PLAN[f"g{b}"][1])
                    for c in range(C):
                        ins = mm(bk(f"g{m}")[:, 0:S], w[:, c, m * P:(m + 1) * P], h1[:, C * u + c, :],
                                 u == 0 and c == 0, u == 3 and c == C - 1)
                    if m == C - 1:
                        used(ins)
                        n_used[0] += 1
                    if u == 3 and m < C - 1:
                        inc_filled(ins, f"g{m}")
                    if u == 3 and m == C - 1:
                        pe.wait_ge(s["unit_used"], n_used[0])
                        bank_done("g7")
                        pe.sem_inc(s["hid_used"], 1)
                    if u == 3:
                        for c in [m - 3] if m < C - 1 else range(m - 3, C):
                            if c < 0:
                                continue
                            for k, (label, sq) in enumerate((("n_fin", sq2), ("n_one", sqg))):
                                if c == 0:
                                    wait_emptied(pe, label)
                                pe.wait_ge(s["sq2_set"], 2 * c + k + 1)
                                ins = mm(bk(label)[:, 0:S], ones[:, :], sq[:, c, :], c == 0, c == C - 1)
                                if c == C - 1:
                                    inc_filled(ins, label)

            wait_unit(pe, "conv")
            w = unit_ap("conv", C, 1024)
            for m in range(CT):
                proj(f"cb{m}", w, CW + m * P, hT, s["h2_set"] if m == 0 else None)
                proj(f"ca{m}", w, m * P, hT, last=(m == CT - 1))
            wait_unit(pe, "qk")
            w = unit_ap("qk", C, 1024)
            pe.wait_ge(s["consts2_in"], 32)

            def q_squares(m):
                if m == 0:
                    wait_emptied(pe, "qs")
                pe.wait_ge(s["qsq_set"], m + 1)
                mm(bk("qs")[0:16, 0:S], selh[:, 16 * m:16 * m + 16], qsq[:, m % 2, :], m == 0, m == 7)\
                    .then_inc(s["pe_link"], 1)

            for m in range(8):
                proj(f"qk{m}", w, m * P, hT, last=(m == 7))
                if m >= 1:
                    q_squares(m - 1)
            q_squares(7)
            pe.wait_ge(s["pe_link"], 8)
            bank_done("qs")
            wait_unit(pe, "v")
            w = unit_ap("v", C, 512)
            def spread(p):
                wait_emptied(pe, f"bc{p}")
                for k in range(2):
                    m = 2 * p + k
                    ins = mm(bk(f"bc{p}")[:, k * S:(k + 1) * S], bsel[:, m * P:(m + 1) * P], rs16, True, True)
                inc_filled(ins, f"bc{p}")

            proj_rows("v0", w, 0, hT, 0)
            pe.wait_ge(s["rs16i_set"], 1)
            spread(0)
            spread(1)
            pe.wait_ge(s["conv_set"], TAPS * (CT - 1))
            pe.wait_ge(s["conv_pool_set"], TAPS - 1)
            wait_emptied(pe, "cm")
            for m in range(CT):
                ins = mm(bk("cm")[:, 0:S], ones[:, :], mix2[:, 4 + m, :], m == 0, m == CT - 1)
            inc_filled(ins, "cm")
            proj_rows("v1", w, 0, hT, 1, last=True)
            for p in range(4):
                pe.wait_ge(s["qn_set"], p + 1)
                wait_emptied(pe, f"rt{p}")
                inc_filled(mm(bk(f"rt{p}"), rot, flat(qk[:, 2 * p:2 * p + 2, :]), True, True), f"rt{p}")
                if p < 2:
                    spread(p + 2)
            pe.wait_ge(s["csq_set"], 1)
            wait_emptied(pe, "cv")
            for m in range(CT):
                ins = mm(bk("cv")[:, 0:S], ones[:, :], csq[:, m, :], m == 0, m == CT - 1)
            inc_filled(ins, "cv")
            pe.wait_ge(s["qf_set"], 4)
            pe.wait_ge(s["v_set"], 2)
            for i in range(MH + 2):
                for j in (0, 1) if i == 0 else (i + 1,):
                    if j < MH:
                        hp, mt = 64 * (j % 2), j // 2
                        wait_emptied(pe, f"tc{j}")
                        for st in range(ST):
                            ins = mm(bk(f"tc{j}")[:, st * S:(st + 1) * S], qk[hp:hp + HD, mt, st * P:(st + 1) * P],
                                     qk[hp:hp + HD, 4 + mt, :], True, True)
                        inc_filled(ins, f"tc{j}")
                if 1 <= i <= MH:
                    j = i - 1
                    b = j % 2
                    pe.wait_ge(s["tp_set"], 2 * j + 2)
                    wait_emptied(pe, f"uT{j}")
                    for kt in range(ST):
                        for st in range(ST):
                            ins = pe.transpose(bk(f"uT{j}")[:, kt * S + st * P:kt * S + (st + 1) * P],
                                               tcb[j % 3][:, st * S + kt * P:st * S + (kt + 1) * P], ident[:, :])
                    inc_filled(ins, f"uT{j}")
                if i >= 2:
                    j = i - 2
                    hp = 64 * (j % 2)
                    label = f"pw{j // 2}"
                    if j % 2 == 0:
                        wait_emptied(pe, label)
                    pe.wait_ge(s["uT_set"], j + 1)
                    for kt in range(ST):
                        ins = mm(bk(label)[hp:hp + HD, 0:S], vn[:, kt, j * HD:(j + 1) * HD],
                                 uTb[:, j % 2, kt * S:(kt + 1) * S], kt == 0, kt == 1)
                    if j % 2:
                        inc_filled(ins, label)

            def mixed2():
                pe.wait_ge(s["mixa_set"], 4)
                pe.wait_ge(s["mixc_set"], 1)

            w0, w1_ = unit_ap("wo2_0", C, 512), unit_ap("wo2_1", C, 512)
            out_proj("z", "n_two", lambda m: ((w0, w1_)[m // 4], (m % 4) * P, m % 4 == 3), mix2, mixed2,
                     sq2, s["sq3_set"], {0: "wo2_0", 4: "wo2_1"})
            wait_emptied(pe, "lg")
            for st in range(ST):
                for c in range(C):
                    if st == 0:
                        pe.wait_ge(s["h3_set"], c + 1)
                    ins = mm(bk("lg")[:, st * NE:(st + 1) * NE], hT[:, c, st * P:(st + 1) * P],
                             wr[:, c * NE:(c + 1) * NE], c == 0, c == C - 1)
            inc_filled(ins, "lg")
            for i in range(4):
                turn(f"hn{i}", lambda k, st: hT[:, 2 * i + k, st * P:(st + 1) * P])
            pe.wait_ge(s["aff_set"], 1)
            wait_emptied(pe, "aT")
            for st in range(ST):
                ins = pe.transpose(bk("aT")[0:NE, st * P:(st + 1) * P], aff[:, st, :], ident[:, :])
            inc_filled(ins, "aT")
            for i in range(4):
                turn(f"xf{i}", lambda k, st: xT[:, 2 * i + k, st * P:(st + 1) * P])
            pe.wait_ge(s["place_set"], 1)
            wait_emptied(pe, "rk")
            for st in range(ST):
                ins = pe.transpose(bk("rk")[:, st * NE:(st + 1) * NE], placeT[:, st * P:(st + 1) * P],
                                   ident[0:NE, 0:NE])
            inc_filled(ins, "rk")
            pe.wait_ge(s["pick_set"], 1)
            pe.wait_ge(s["hnat_set"], 8)
            for b in range(8):
                n = max(u + 1 for bb_, u in PLAN.values() if bb_ == b)
                pe.wait_ge(emptied[b], n)

            pe.sem_inc(s["pgT_full"], 1)
            pe.sem_inc(s["sc_full"], 1)
            with pe.Fori(0, NE) as e:
                pe.wait_ge(s["xe_set"], 1 + e)
                for c in range(C):
                    for st in range(ST):
                        ins = mm(ps[:, 7, c * CAP:(c + 1) * CAP],
                                 hnat[:, st, c * P:(c + 1) * P],
                                 pick[:, st, bass.ds(e * CAP, CAP)], st == 0, st == 1)
                ins.then_inc(s["xe_full"], 1)
                pe.wait_ge(s["pgs_set"], e + 1)
                pe.wait_ge(s["ye_set"], 1 + e)
                for st in range(ST):
                    ins = pe.transpose(ps[:, 4, st * P:(st + 1) * P], pgs[:, st, :], ident[:, :])
                ins.then_inc(s["pgT_full"], 1)
                pe.wait_ge(s["xe_set"], e + 2)
                for mat, (full, bank) in enumerate(((s["h1_full"], 0), (s["h3_full"], 2))):
                    pe.wait_ge(s["he_set"], 1 + 2 * e)
                    for c in range(C):
                        q = mat * C + c
                        slot = (9 + q) % NSLOT
                        pe.wait_ge(chunk_in[slot], 32 * e + 16 * (q // NSLOT + 1))
                        w = ring[:, slot * SLOT:(slot + 1) * SLOT]
                        for half in range(2):
                            for j in range(4):
                                c0 = j * FG + half * FH
                                ins = mm(ps[32 * j:32 * j + CAP, bank + half, 0:FH], xe[:, c, :], w[:, c0:c0 + FH],
                                         c == 0, c == C - 1)
                        ins.then_inc(s["w_used"], 1)
                    pe.wait_ge(s["w_used"], NCHUNK * e + (mat + 1) * C)
                    pe.sem_inc(full, 1)
                pe.wait_ge(s["hTe_set"], e + 1)
                pe.wait_ge(s["pgT_set"], e + 1)
                w2v = ring[:, 1 * SLOT:9 * SLOT].rearrange("p (r n) -> p r n", r=FR)
                got = 0
                for r in range(FR):
                    while got * SLOT < (r + 1) * D:
                        q = 2 * C + got
                        slot = (9 + q) % NSLOT
                        pe.wait_ge(chunk_in[slot], 32 * e + 16 * (q // NSLOT + 1))
                        got += 1
                    for j in range(4):
                        ins = mm(ps[32 * j:32 * j + CAP, 4, 0:DG], hTe[:, r, :], w2v[:, r, j * DG:(j + 1) * DG],
                                 r == 0, r == FR - 1)
                    if any((k * SLOT - 1) // D == r for k in range(1, C + 1)):
                        ins.then_inc(s["w_used"], 1)
                pe.wait_ge(s["w_used"], NCHUNK * e + NCHUNK)
                pe.sem_inc(s["ye_full"], 1)
                pe.wait_ge(s["ye_set"], e + 2)
                pe.wait_ge(s["pgT_set"], e + 1)
                for j in range(4):
                    if j < 2:
                        pe.wait_ge(s["sc_used"], 1 + 4 * e)
                    else:
                        pe.wait_ge(s["sc_used"], 4 * e + j)
                    for st in range(ST):
                        ins = mm(ps[:, 5 + j % 2, st * DG:(st + 1) * DG], pgT[32 * j:32 * j + CAP, st * P:(st + 1) * P],
                                 ye[32 * j:32 * j + CAP, :], True, True)
                    ins.then_inc(s["sc_full"], 1)


def S_at(Sst, n, mt):
    return Sst[:, n, mt, :]


def laid_out(given):
    cols = []
    for name, (_, n) in VEC.items():
        v = given[name].reshape(-1)
        cols.append(np.concatenate([v, v]).reshape(1, P) if v.size == HD else v.reshape(n, P))
    vectors = np.concatenate(cols).T
    taps = given["conv_dw_w_2"].reshape(TAPS, CT, P).transpose(2, 1, 0).reshape(P, CT * TAPS)
    router = given["w_router_2"].reshape(C, P, NE).transpose(1, 0, 2).reshape(P, C * NE)
    table0 = np.ascontiguousarray(np.concatenate([vectors, taps, router], axis=1))
    x_turned = np.ascontiguousarray(given["x"].reshape(S, C, P).transpose(2, 1, 0))
    return {"table0": table0, "x_turned": x_turned}


def tables():
    f = np.float32
    p = np.arange(P)
    n = np.arange(S)
    ratio = np.maximum(n, 1).astype(f) / f(16)
    large = 16 + (np.log(ratio) / f(np.log(8.0)) * f(16)).astype(np.int32)
    bucket = np.where(n < 16, n, np.minimum(large, BUCKETS - 1))
    t1 = np.zeros((P, P + 384 + P), f)
    t1[:, P + 384:] = np.eye(P)[::-1]
    t1[:, 0:P] = np.eye(P)
    dist = S - 1 - np.arange(S)
    t1[bucket[dist], P + np.arange(S)] = 1.0
    half = HD // 2
    inv = (f(10000.0) ** (-np.arange(half, dtype=f) / f(half))).astype(f)
    ang = (np.arange(S, dtype=f)[:, None] * inv[None, :]).astype(f)
    cos, sin = np.cos(ang).T, np.sin(ang).T
    t2 = np.zeros((P, 2816), f)
    t2[:, 0:512] = np.tile(cos, (4, 2))
    t2[:, 512:1024] = np.tile(sin, (4, 2))
    q = (np.arange(ST)[None, :, None] * P + p[:, None, None])
    diff = q - np.arange(S)[None, None, :]
    count = (abs(diff) <= 64).astype(f) + (diff % 4 == 0) + (diff % 16 == 0)
    t2[:, 1024:1536] = count.reshape(P, 512)
    for i in range(P):
        if i % HD < half:
            t2[i + half, 1536 + i] = -1.0
        else:
            t2[i - half, 1536 + i] = 1.0
    for m in range(8):
        for i in range(P):
            t2[i, 1664 + 16 * m + 2 * m + i // HD] = 1.0
            t2[2 * m + i // HD, 1792 + m * P + i] = 1.0
    t3 = np.tile(np.arange(1, CAP + 1, dtype=f), (P, 1))
    return {"table1": t1, "table2": t2, "table3": t3}


_INS = ["x", "c", "w_ada", "b_ada", "g_mix", "w_in", "w_gla_gate", "b_gla_gate", "g_gla_out", "rel_bias", "w_out",
        "g_mlp", "w_ff1", "w_ff2", "g_final", "norm1_g_2", "w_in_2", "q_norm_g_2", "k_norm_g_2", "conv_dw_w_2",
        "conv_dw_b_2", "conv_ln_g_2", "conv_ln_b_2", "w_out_2", "norm2_g_2", "w_router_2", "w1_2", "w3_2", "w2_2"]
_LAYERED = ("w_ada", "w_in", "w_gla_gate", "w_out", "w_ff1", "w_ff2")


def kernel(**inputs):
    import concourse.bacc as bacc
    from concourse.bass_utils import run_bass_kernel_spmd

    nc = bacc.Bacc("TRN2", target_bir_lowering=False, num_devices=1)
    arrays, args = {}, {}
    given = {name: np.ascontiguousarray(inputs[name]) for name in _INS}
    given.update(laid_out(given))
    given.update(tables())
    for name in ("x", "conv_dw_w_2", "w_router_2", *VEC):
        del given[name]
    for name, a in given.items():
        arrays[f"in_{name}"] = a
        ap = nc.dram_tensor(f"in_{name}", a.shape, mybir.dt.from_np(a.dtype), kind="ExternalInput").ap()
        args[name] = ap[0] if name in _LAYERED else ap
    out = nc.dram_tensor("out_0", (1, S, D), F32, kind="ExternalOutput").ap()
    rel_dram = nc.dram_tensor("rel_rows", (MH, 384), F32, kind="Internal").ap()
    build(nc, args, out, rel_dram)
    r = run_bass_kernel_spmd(nc, [arrays], core_ids=[0])
    return r.results[0]["out_0"]
```
